# Optimizing a Trainium2 kernel written in Bass

```python
import math
import jax
import jax.numpy as jnp
from jax import lax
import numpy as np

D_MODEL = 1024
BATCH = 1
SEQ = 512
DEPTH = 2
DEC_BATCH = 8
DEC_SEQ = 1
PAST_LEN = 4096
PAGE_SIZE = 128

N_MIX_LAYERS = (DEPTH + 1) // 2
N_CONV_LAYERS = DEPTH // 2

A_HEADS = 8
A_KV_HEADS = 2
A_GROUP = A_HEADS // A_KV_HEADS
A_HEAD_DIM = 64
WINDOW = 128
REL_BUCKETS = 32
REL_MAX_DIST = 128

B_HEADS = 4
B_DK = 64
B_DV = 128
B_CONV = 4
MLSTM_CHUNK = 64
FORGET_BIAS_LO = 3.0
FORGET_BIAS_HI = 6.0

C_WIDTH = D_MODEL
C_KERNEL = 31

N_GROUPS = 4
EXPERTS_PER_GROUP = 8
N_EXPERTS = N_GROUPS * EXPERTS_PER_GROUP
TOP_K = 2
EXPERT_FF = D_MODEL // 2
EXPERT_BLOCK = 128

EPS = 1e-6

A_Q = A_HEADS * A_HEAD_DIM
A_KV = A_KV_HEADS * A_HEAD_DIM
B_QK = B_HEADS * B_DK
B_V = B_HEADS * B_DV
MIX_WIDTH = A_Q + B_V
IN_COLS = A_Q + 2 * A_KV + 2 * B_QK + B_V + 2 * B_HEADS + B_V
SPLITS = (A_Q, A_Q + A_KV, A_Q + 2 * A_KV, A_Q + 2 * A_KV + 2 * B_QK,
          A_Q + 2 * A_KV + 2 * B_QK + B_V, A_Q + 2 * A_KV + 2 * B_QK + B_V + 2 * B_HEADS)

kernel_name = 'hybrid_swa_mlstm_conformer_hmoe_step'

def rmsnorm(x, g):
    xf = x.astype(jnp.float32)
    y = xf * lax.rsqrt(jnp.mean(xf * xf, axis=-1, keepdims=True) + EPS)
    return (y * g.astype(jnp.float32)).astype(x.dtype)

def layernorm(x, g, b):
    xf = x.astype(jnp.float32)
    xc = xf - jnp.mean(xf, axis=-1, keepdims=True)
    y = xc * lax.rsqrt(jnp.mean(xc * xc, axis=-1, keepdims=True) + EPS)
    return (y * g.astype(jnp.float32) + b.astype(jnp.float32)).astype(x.dtype)

def causal_dwconv(x_ext, w):
    ch = x_ext.shape[-1]
    return lax.conv_general_dilated(x_ext, w.astype(x_ext.dtype)[:, None, :], window_strides=(1,), padding='VALID',
                                    dimension_numbers=('NWC', 'WIO', 'NWC'), feature_group_count=ch)

def t5_bucket(dist):
    exact = REL_BUCKETS // 2
    d = jnp.maximum(dist, 0)
    large = exact + (jnp.log(jnp.maximum(d, 1).astype(jnp.float32) / exact)
                     / math.log(REL_MAX_DIST / exact) * (REL_BUCKETS - exact)).astype(jnp.int32)
    return jnp.where(d < exact, d, jnp.minimum(large, REL_BUCKETS - 1))

def window_attention(q, k, v, dist, valid, sinks, rel_table):
    logits = jnp.einsum('bnqkgd,bnskd->bnkgqs', q, k).astype(jnp.float32) * (A_HEAD_DIM ** -0.5)
    bias = rel_table.astype(jnp.float32)[t5_bucket(dist)]
    bias = jnp.moveaxis(bias, -1, 0).reshape(A_KV_HEADS, A_GROUP, dist.shape[0], dist.shape[1])
    logits = jnp.where(valid[:, None, None], logits + bias, -jnp.inf)
    sink = sinks.astype(jnp.float32).reshape(A_KV_HEADS, A_GROUP, 1, 1)
    mx = jnp.maximum(jnp.max(logits, axis=-1, keepdims=True), sink)
    p = jnp.exp(logits - mx)
    probs = p / (jnp.sum(p, axis=-1, keepdims=True) + jnp.exp(sink - mx))
    return jnp.einsum('bnkgqs,bnskd->bnqkgd', probs.astype(v.dtype), v)

def mlstm_chunk(carry, inp):
    c0, n0, m0 = carry
    q, k, v, ig, lf = inp
    L = q.shape[2]
    b = jnp.cumsum(lf, axis=-1)
    a = b + m0[..., None]
    causal = jnp.tril(jnp.ones((L, L), dtype=bool))
    d = jnp.where(causal, b[..., :, None] - b[..., None, :] + ig[..., None, :], -jnp.inf)
    m = jnp.maximum(a, jnp.max(d, axis=-1))
    dw = jnp.exp(d - m[..., None])
    aw = jnp.exp(a - m)
    s = jnp.einsum('bhtd,bhsd->bhts', q, k) * dw
    num = jnp.einsum('bhts,bhsv->bhtv', s, v) + aw[..., None] * jnp.einsum('bhtd,bhdv->bhtv', q, c0)
    den = jnp.sum(s, axis=-1) + aw * jnp.einsum('bhtd,bhd->bht', q, n0)
    h = num / jnp.maximum(jnp.abs(den), jnp.exp(-m))[..., None]
    w_last = dw[..., -1, :]
    decay = aw[..., -1]
    c1 = decay[..., None, None] * c0 + jnp.einsum('bhs,bhsd,bhsv->bhdv', w_last, k, v)
    n1 = decay[..., None] * n0 + jnp.einsum('bhs,bhsd->bhd', w_last, k)
    return (c1, n1, m[..., -1]), h

def ab_mixer(h, state, w_in, b_gates, w_qk_conv, sinks, rel_table, g_mnorm, w_out, prompt):
    bsz, T, _ = h.shape
    z = h @ w_in
    qa, ka, va, qk_pre, v_pre, gates, og = jnp.split(z, SPLITS, axis=-1)
    qa = qa.reshape(bsz, T, A_KV_HEADS, A_GROUP, A_HEAD_DIM)
    ka = ka.reshape(bsz, T, A_KV_HEADS, A_HEAD_DIM)
    va = va.reshape(bsz, T, A_KV_HEADS, A_HEAD_DIM)
    if prompt:
        nb = T // WINDOW
        qb = qa.reshape(bsz, nb, WINDOW, A_KV_HEADS, A_GROUP, A_HEAD_DIM)
        kb = ka.reshape(bsz, nb, WINDOW, A_KV_HEADS, A_HEAD_DIM)
        vb = va.reshape(bsz, nb, WINDOW, A_KV_HEADS, A_HEAD_DIM)

        def band(t):
            prev = jnp.concatenate([jnp.zeros_like(t[:, :1]), t[:, :-1]], axis=1)
            return jnp.concatenate([prev, t], axis=2)

        dist = WINDOW + jnp.arange(WINDOW)[:, None] - jnp.arange(2 * WINDOW)[None, :]
        kpos = (jnp.arange(nb)[:, None] - 1) * WINDOW + jnp.arange(2 * WINDOW)[None, :]
        valid = ((dist >= 0) & (dist <= WINDOW))[None] & (kpos >= 0)[:, None, :]
        att = window_attention(qb, band(kb), band(vb), dist, valid, sinks, rel_table)
        new_k, new_v = ka[:, -WINDOW:], va[:, -WINDOW:]
        qk_ext = jnp.pad(qk_pre, ((0, 0), (B_CONV - 1, 0), (0, 0)))
    else:
        win_k, win_v, c0, n0, m0, conv_buf = state
        k_all = jnp.concatenate([win_k.astype(ka.dtype), ka], axis=1)
        v_all = jnp.concatenate([win_v.astype(va.dtype), va], axis=1)
        n_buf = win_k.shape[1]
        dist = n_buf + jnp.arange(T)[:, None] - jnp.arange(n_buf + T)[None, :]
        valid = ((dist >= 0) & (dist <= WINDOW))[None]
        att = window_attention(qa[:, None], k_all[:, None], v_all[:, None], dist, valid, sinks, rel_table)[:, 0]
        new_k, new_v = k_all[:, -n_buf:], v_all[:, -n_buf:]
        qk_ext = jnp.concatenate([conv_buf.astype(qk_pre.dtype), qk_pre], axis=1)
    att = att.reshape(bsz, T, A_Q)

    qk = jax.nn.silu(causal_dwconv(qk_ext, w_qk_conv))
    new_conv = qk_ext[:, -(B_CONV - 1):]
    q, k = jnp.split(qk.astype(jnp.float32), 2, axis=-1)

    def to_heads(t, dh):
        return t.reshape(bsz, T, B_HEADS, dh).transpose(0, 2, 1, 3)

    q = to_heads(q, B_DK)
    k = to_heads(k, B_DK) * (B_DK ** -0.5)
    v = to_heads(v_pre.astype(jnp.float32), B_DV)
    gates = gates.astype(jnp.float32) + b_gates.astype(jnp.float32)
    ig = gates[..., :B_HEADS].transpose(0, 2, 1)
    lf = jax.nn.log_sigmoid(gates[..., B_HEADS:]).transpose(0, 2, 1)
    if prompt:
        nc = T // MLSTM_CHUNK

        def chunks(t):
            return jnp.moveaxis(t.reshape((bsz, B_HEADS, nc, MLSTM_CHUNK) + t.shape[3:]), 2, 0)

        init = (jnp.zeros((bsz, B_HEADS, B_DK, B_DV), jnp.float32),
                jnp.zeros((bsz, B_HEADS, B_DK), jnp.float32),
                jnp.full((bsz, B_HEADS), -jnp.inf, jnp.float32))
        (c1, n1, m1), hs = lax.scan(mlstm_chunk, init, (chunks(q), chunks(k), chunks(v), chunks(ig), chunks(lf)))
        hs = jnp.moveaxis(hs, 0, 2).reshape(bsz, B_HEADS, T, B_DV)
    else:
        carry = (c0.astype(jnp.float32), n0.astype(jnp.float32), m0.astype(jnp.float32))
        (c1, n1, m1), hs = mlstm_chunk(carry, (q, k, v, ig, lf))
    hs = hs.transpose(0, 2, 1, 3)
    hs = hs * lax.rsqrt(jnp.mean(hs * hs, axis=-1, keepdims=True) + EPS) * g_mnorm.astype(jnp.float32).reshape(B_HEADS, B_DV)
    out_b = (jax.nn.sigmoid(og.astype(jnp.float32)) * hs.reshape(bsz, T, B_V)).astype(h.dtype)

    y = jnp.concatenate([att.astype(h.dtype), out_b], axis=-1) @ w_out
    dt = h.dtype
    return y, (new_k, new_v, c1.astype(dt), n1.astype(dt), m1.astype(dt), new_conv)

def conformer_conv(h, conv_buf, w_pw1, b_pw1, w_dw, b_dw, ln_g, ln_b, w_pw2, b_pw2, prompt):
    u = h @ w_pw1 + b_pw1
    a, gate = jnp.split(u, 2, axis=-1)
    u = a * jax.nn.sigmoid(gate)
    if prompt:
        ext = jnp.pad(u, ((0, 0), (C_KERNEL - 1, 0), (0, 0)))
    else:
        ext = jnp.concatenate([conv_buf.astype(u.dtype), u], axis=1)
    y = causal_dwconv(ext, w_dw) + b_dw
    y = jax.nn.silu(layernorm(y, ln_g, ln_b))
    return y @ w_pw2 + b_pw2, ext[:, -(C_KERNEL - 1):]

def hier_moe(x, w_rg, b_rg, w_re, b_re, w_eg, w_eu, w_ed):
    bsz, T, D = x.shape
    n_tok = bsz * T
    xt = x.reshape(n_tok, D)
    xf = xt.astype(jnp.float32)
    g_logits = xf @ w_rg.astype(jnp.float32) + b_rg.astype(jnp.float32)
    g_idx = jnp.argmax(g_logits, axis=-1)
    g_gate = jnp.take_along_axis(jax.nn.softmax(g_logits, axis=-1), g_idx[:, None], axis=1)
    e_logits = jnp.einsum('nd,gde->nge', xf, w_re.astype(jnp.float32)) + b_re.astype(jnp.float32)
    e_logits = jnp.take_along_axis(e_logits, g_idx[:, None, None], axis=1)[:, 0]
    top_v, top_j = lax.top_k(e_logits, TOP_K)
    gate = jax.nn.softmax(top_v, axis=-1) * g_gate
    expert = (g_idx[:, None] * EXPERTS_PER_GROUP + top_j).astype(jnp.int32)

    n_assign = n_tok * TOP_K
    e_flat = expert.reshape(-1)
    tok_flat = jnp.repeat(jnp.arange(n_tok, dtype=jnp.int32), TOP_K)
    w_flat = gate.reshape(-1)
    order = jnp.argsort(e_flat)
    e_s, tok_s, w_s = e_flat[order], tok_flat[order], w_flat[order]
    counts = jnp.bincount(e_flat, length=N_EXPERTS).astype(jnp.int32)
    starts = jnp.cumsum(counts) - counts
    padded = (counts + EXPERT_BLOCK - 1) // EXPERT_BLOCK * EXPERT_BLOCK
    pends = jnp.cumsum(padded)
    pstarts = pends - padded
    n_blocks = (n_assign + N_EXPERTS * (EXPERT_BLOCK - 1)) // EXPERT_BLOCK
    n_slots = n_blocks * EXPERT_BLOCK
    dest = pstarts[e_s] + jnp.arange(n_assign, dtype=jnp.int32) - starts[e_s]
    slot_tok = jnp.full((n_slots,), n_tok, jnp.int32).at[dest].set(tok_s)
    slot_w = jnp.zeros((n_slots,), jnp.float32).at[dest].set(w_s)
    block_e = jnp.minimum(jnp.searchsorted(pends, jnp.arange(n_blocks, dtype=jnp.int32) * EXPERT_BLOCK, side='right'),
                          N_EXPERTS - 1)
    x_pad = jnp.concatenate([xt, jnp.zeros((1, D), xt.dtype)], axis=0)
    xb = x_pad[slot_tok].reshape(n_blocks, EXPERT_BLOCK, D)

    def expert_block(args):
        xblk, e = args
        hid = jax.nn.silu(xblk @ w_eg[e]) * (xblk @ w_eu[e])
        return hid @ w_ed[e]

    yb = lax.map(expert_block, (xb, block_e)).reshape(n_slots, D)
    out = jnp.zeros((n_tok + 1, D), jnp.float32).at[slot_tok].add(yb.astype(jnp.float32) * slot_w[:, None])[:n_tok]
    return out.astype(x.dtype).reshape(bsz, T, D)

def trunk(x, caches, weights, prompt):
    (norm_mix, norm_ffn, norm_final, rel_bias_table, w_in_mix, b_mlstm_gates, w_mlstm_qk_conv, attn_sinks,
     g_mlstm_norm, w_out_mix, w_pw1, b_pw1, w_dw, b_dw, ln_conv_g, ln_conv_b, w_pw2, b_pw2,
     w_router_group, b_router_group, w_router_expert, b_router_expert, w_expert_gate, w_expert_up,
     w_expert_down) = weights
    mix_states, conv_states = [], []
    for layer in range(DEPTH):
        li = layer // 2
        h = rmsnorm(x, norm_mix[layer])
        if layer % 2 == 0:
            st = None if prompt else (caches[0][li], caches[1][li], caches[2][li], caches[3][li], caches[4][li], caches[5][li])
            y, ns = ab_mixer(h, st, w_in_mix[li], b_mlstm_gates[li], w_mlstm_qk_conv[li], attn_sinks[li],
                             rel_bias_table, g_mlstm_norm[li], w_out_mix[li], prompt)
            mix_states.append(ns)
        else:
            y, nbuf = conformer_conv(h, None if prompt else caches[6][li], w_pw1[li], b_pw1[li], w_dw[li], b_dw[li],
                                     ln_conv_g[li], ln_conv_b[li], w_pw2[li], b_pw2[li], prompt)
            conv_states.append(nbuf)
        x = x + y
        x = x + hier_moe(rmsnorm(x, norm_ffn[layer]), w_router_group[layer], b_router_group[layer],
                         w_router_expert[layer], b_router_expert[layer], w_expert_gate[layer],
                         w_expert_up[layer], w_expert_down[layer])
    wk, wv, mc, mn, mm, mconv = (jnp.stack(s) for s in zip(*mix_states))
    return (rmsnorm(x, norm_final), wk, wv, mc, mn, mm, mconv, jnp.stack(conv_states))

def setup_inputs(seed: int = 0) -> dict:
    key = jax.random.key(seed)
    it = iter(jax.random.split(key, 40))

    def nrm(shape, scale):
        return jax.random.normal(next(it), shape, jnp.float32) * scale

    win_buf = min(WINDOW, PAST_LEN)
    forget_bias = jnp.broadcast_to(jnp.linspace(FORGET_BIAS_LO, FORGET_BIAS_HI, B_HEADS), (N_MIX_LAYERS, B_HEADS))
    return {
        'x_prompt': nrm((BATCH, SEQ, D_MODEL), 1.0),
        'x_sample': nrm((DEC_BATCH, DEC_SEQ, D_MODEL), 1.0),
        'cache_win_k': nrm((N_MIX_LAYERS, DEC_BATCH, win_buf, A_KV_HEADS, A_HEAD_DIM), 1.0),
        'cache_win_v': nrm((N_MIX_LAYERS, DEC_BATCH, win_buf, A_KV_HEADS, A_HEAD_DIM), 1.0),
        'state_mlstm_c': nrm((N_MIX_LAYERS, DEC_BATCH, B_HEADS, B_DK, B_DV), 0.5),
        'state_mlstm_n': nrm((N_MIX_LAYERS, DEC_BATCH, B_HEADS, B_DK), 0.5),
        'state_mlstm_m': 1.0 + nrm((N_MIX_LAYERS, DEC_BATCH, B_HEADS), 0.5),
        'state_mlstm_conv': nrm((N_MIX_LAYERS, DEC_BATCH, B_CONV - 1, 2 * B_QK), 1.0),
        'state_conv': nrm((N_CONV_LAYERS, DEC_BATCH, C_KERNEL - 1, C_WIDTH), 0.5),
        'norm_mix': 1.0 + nrm((DEPTH, D_MODEL), 0.02),
        'norm_ffn': 1.0 + nrm((DEPTH, D_MODEL), 0.02),
        'norm_final': 1.0 + nrm((D_MODEL,), 0.02),
        'rel_bias_table': nrm((REL_BUCKETS, A_HEADS), 0.5),
        'w_in_mix': nrm((N_MIX_LAYERS, D_MODEL, IN_COLS), D_MODEL ** -0.5),
        'b_mlstm_gates': jnp.concatenate([nrm((N_MIX_LAYERS, B_HEADS), 0.1),
                                          forget_bias + nrm((N_MIX_LAYERS, B_HEADS), 0.1)], axis=-1),
        'w_mlstm_qk_conv': nrm((N_MIX_LAYERS, B_CONV, 2 * B_QK), B_CONV ** -0.5),
        'attn_sinks': nrm((N_MIX_LAYERS, A_HEADS), 0.5),
        'g_mlstm_norm': 1.0 + nrm((N_MIX_LAYERS, B_V), 0.02),
        'w_out_mix': nrm((N_MIX_LAYERS, MIX_WIDTH, D_MODEL), MIX_WIDTH ** -0.5),
        'w_pw1': nrm((N_CONV_LAYERS, D_MODEL, 2 * C_WIDTH), D_MODEL ** -0.5),
        'b_pw1': nrm((N_CONV_LAYERS, 2 * C_WIDTH), 0.02),
        'w_dw': nrm((N_CONV_LAYERS, C_KERNEL, C_WIDTH), C_KERNEL ** -0.5),
        'b_dw': nrm((N_CONV_LAYERS, C_WIDTH), 0.02),
        'ln_conv_g': 1.0 + nrm((N_CONV_LAYERS, C_WIDTH), 0.02),
        'ln_conv_b': nrm((N_CONV_LAYERS, C_WIDTH), 0.02),
        'w_pw2': nrm((N_CONV_LAYERS, C_WIDTH, D_MODEL), C_WIDTH ** -0.5),
        'b_pw2': nrm((N_CONV_LAYERS, D_MODEL), 0.02),
        'w_router_group': nrm((DEPTH, D_MODEL, N_GROUPS), D_MODEL ** -0.5),
        'b_router_group': nrm((DEPTH, N_GROUPS), 0.01),
        'w_router_expert': nrm((DEPTH, N_GROUPS, D_MODEL, EXPERTS_PER_GROUP), D_MODEL ** -0.5),
        'b_router_expert': nrm((DEPTH, N_GROUPS, EXPERTS_PER_GROUP), 0.01),
        'w_expert_gate': nrm((DEPTH, N_EXPERTS, D_MODEL, EXPERT_FF), D_MODEL ** -0.5),
        'w_expert_up': nrm((DEPTH, N_EXPERTS, D_MODEL, EXPERT_FF), D_MODEL ** -0.5),
        'w_expert_down': nrm((DEPTH, N_EXPERTS, EXPERT_FF, D_MODEL), EXPERT_FF ** -0.5),
    }

def reference(x_prompt, x_sample, cache_win_k, cache_win_v, state_mlstm_c, state_mlstm_n, state_mlstm_m,
              state_mlstm_conv, state_conv, norm_mix, norm_ffn, norm_final, rel_bias_table, w_in_mix,
              b_mlstm_gates, w_mlstm_qk_conv, attn_sinks, g_mlstm_norm, w_out_mix, w_pw1, b_pw1, w_dw, b_dw,
              ln_conv_g, ln_conv_b, w_pw2, b_pw2, w_router_group, b_router_group, w_router_expert,
              b_router_expert, w_expert_gate, w_expert_up, w_expert_down):
    weights = (norm_mix, norm_ffn, norm_final, rel_bias_table, w_in_mix, b_mlstm_gates, w_mlstm_qk_conv,
               attn_sinks, g_mlstm_norm, w_out_mix, w_pw1, b_pw1, w_dw, b_dw, ln_conv_g, ln_conv_b, w_pw2,
               b_pw2, w_router_group, b_router_group, w_router_expert, b_router_expert, w_expert_gate,
               w_expert_up, w_expert_down)
    caches = (cache_win_k, cache_win_v, state_mlstm_c, state_mlstm_n, state_mlstm_m, state_mlstm_conv, state_conv)
    y_prompt, p_wk, p_wv, p_c, p_n, p_m, p_mconv, p_conv = trunk(x_prompt, None, weights, True)
    y_sample, s_wk, s_wv, s_c, s_n, s_m, s_mconv, s_conv = trunk(x_sample, caches, weights, False)
    return (y_prompt, y_sample, p_wk, p_wv, p_c, p_n, p_m, p_mconv, p_conv,
            s_wk, s_wv, s_c, s_n, s_m, s_mconv, s_conv)


_drawn_inputs = setup_inputs


def setup_inputs(seed=0):
    import zlib

    import numpy as np

    out = dict(_drawn_inputs(seed))
    spreads = {}
    factors = {'norm_final': 22.489, 'attn_sinks': 8.0, 'b_router_expert': 3.094, 'ln_conv_b': 2.82}
    for name, (base, spread) in spreads.items():
        noise = np.random.default_rng([zlib.crc32(name.encode()), seed]).standard_normal(out[name].shape)
        drawn = base * np.exp(spread * noise) if base else spread * noise
        out[name] = jnp.asarray(drawn.astype(out[name].dtype))
    for name, factor in factors.items():
        out[name] = (out[name] * factor).astype(out[name].dtype)
    return out
```

```python
import concourse.bass as bass
from concourse import mybir
from contextlib import ExitStack
import numpy as np

D = 1024
KT = D // 128
NP_, NS_ = 512, 8
TT = NP_ // 128
NT = TT + 1
TOK = NP_ + NS_
AH, AKV, HD, WIN = 8, 2, 64, 128
BH, DK, DV, CONV = 4, 64, 128, 4
VA = DV + 1
LCH = 128
CK = 31
NG, EG, NE, FF = 4, 8, 32, 512
FT = FF // 128
CAP = 96
PASSES = -(-TOK // CAP)
SKIP = 4096.0
EPS = 1e-6
BIG = 1e30
YROWS = 2 * TOK

C_QA, C_KA, C_VA, C_QK, C_V, C_G, C_OG = 0, 512, 640, 768, 1280, 1792, 1800
NCT = 640 + 512
NCN = 136 + 512 + 512


def constants():
    c = {}
    p = np.arange(128)[:, None]
    f = np.arange(128)[None, :]
    c["ident"] = (p == f) * 1.0
    c["before"] = (p < f) * 1.0
    c["count"] = np.broadcast_to(f * 1.0, (128, 128))
    c["ones"] = np.ones((128, 128))
    c["part"] = p * 1.0
    c["samp"] = (p < NS_) * 1.0
    late = np.where(p <= f, 0.0, BIG)
    c["late"] = late
    sel = np.zeros((128, BH, 128))
    half = np.zeros((128, BH, 128))
    for h in range(BH):
        sel[h, h, :] = 1.0
        half[h, h, (h % 2) * 64:(h % 2) * 64 + 64] = 1.0
    c["sel"] = sel.reshape(128, -1)
    c["half"] = half.reshape(128, -1)
    oh = np.zeros((128, 384))
    for i in range(384):
        dist = 2 * WIN - 1 - i
        if 0 <= dist <= WIN:
            if dist < 16:
                b = dist
            else:
                b = min(16 + int(np.float32(np.log(np.float32(dist) / np.float32(16))) / np.float32(np.log(8.0)) * np.float32(16)), 31)
            oh[b, i] = 1.0
        else:
            oh[32, i] = 1.0
    c["bucket"] = oh
    return c


KEEP = ["ident", "before", "count", "ones", "part", "samp"]
MIXC = ["late", "sel", "half", "bucket"]


def const_layout(names):
    c, at, out = constants(), 0, {}
    for n in names:
        out[n] = (at, c[n].shape[1])
        at += c[n].shape[1]
    return out, at


def build(nc, A, O):
    f32, i32, u32 = mybir.dt.float32, mybir.dt.int32, mybir.dt.uint32
    ALU = mybir.AluOpType
    ACT = mybir.ActivationFunctionType
    AX = mybir.AxisListType.X
    ctx = ExitStack()
    with ctx:
        ctx.enter_context(nc.allow_non_contiguous_dma(reason="small per-channel vectors and states"))

        def sb(name, shape, dt=f32):
            return ctx.enter_context(nc.sbuf_tensor(name, shape, dt))

        scope = [ctx]

        def sem(name):
            handle = scope[0].enter_context(nc.semaphore(name))
            (lasting if scope[0] is ctx else part_sems).append(handle)
            return handle

        part_sems, lasting = [], []
        SOFT = 13

        def pool_sem():
            soft_given[0] += 1
            return soft[soft_given[0] - 1]

        soft_given = [0]

        def part_begins():
            soft_given[0] = 0
            scope[0] = ExitStack()
            scope[0].__enter__()

        def part_ends():
            nums = sorted(x.num for x in soft + part_sems)
            assert not [x.num for x in lasting if nums[0] <= x.num <= nums[-1]]
            nc.gpsimd.dma_reset(range(soft[0].num, soft[-1].num + 1))
            nc.all_engine_barrier(sems_to_clear=range(nums[0], nums[-1] + 1))
            scope[0].close()
            part_sems.clear()

        EXP = 3 * KT * FF
        R = sb("ring", [128, 3 * EXP])
        X = sb("x", [128, NT, D])
        AR = sb("arena", [128, 10240])
        klay, kw = const_layout(KEEP)
        mlay, mw = const_layout(MIXC)
        KC = sb("keep", [128, kw])
        P = ctx.enter_context(nc.psum_tensor("psum", [128, 8, 512], f32))
        SM = sb("small", [128, 256])

        def view(t, at, *dims):
            n = int(np.prod(dims))
            v = t[:, at:at + n]
            if len(dims) == 1:
                return v
            names = "abcd"[:len(dims)]
            return v.rearrange(f"p ({' '.join(names)}) -> p {' '.join(names)}",
                               **{k: d for k, d in zip(names, dims)})

        def const(n):
            at, w = klay[n]
            return KC[:, at:at + w]

        ident, before, count_row, ones, part, samp = (const(n) for n in KEEP)

        h_dram = nc.dram_tensor("h_rows", (TOK, D), f32, kind="Internal").ap()
        y_dram = nc.dram_tensor("y_rows", (YROWS, D), f32, kind="Internal").ap()
        g_dram = nc.dram_tensor("bias_line", (AH, 128 * 386), f32, kind="Internal").ap()

        def rows(t):
            return NS_ if t == TT else 128

        keep_in = sem("keep_in")
        small_set = sem("small_set")
        pool_steps = sem("pool_steps")
        x_in = [sem(f"x_in{t}") for t in range(NT)]
        dve_seq, act_seq, pool_seq = sem("dve_seq"), sem("act_seq"), sem("pool_seq")
        out_sp, out_pool = sem("out_sp"), sem("out_pool")
        stores = {"sp": 0, "pool": 0}

        class Chain:
            def __init__(self, eng, s):
                self.eng, self.s, self.n, self.base = eng, s, 0, 0

            def __call__(self, ins):
                self.n += 1
                ins.then_inc(self.s, 1)
                self.eng.wait_ge(self.s, self.base + self.n)

        n_gain_in, n_squares, n_means, n_roots, n_h_ready, n_turned, n_copied = (
            sem(f"norm_{x}") for x in "gain_in squares means roots h_ready turned copied".split())
        n_stored = [sem(f"norm_stored{j}") for j in range(2)]
        HALVES = 2 * TT + 1
        NORM_STORES = [False, True, False, True, False]

        class Norm:
            def __init__(self, n, gain, HT, HN, G, JUNK, store, wait_x):
                self.n, self.gain, self.HT, self.HN, self.G, self.JUNK, self.store, self.wait_x = n, gain, HT, HN, G, JUNK, store, wait_x
                self.prior_stores = sum(1 for m in NORM_STORES[:n] if m)

            def at(self, count, per):
                return self.n * per + count

            def at_store(self, t):
                return 16 * (self.prior_stores * ((NT + 1 - t % 2) // 2) + t // 2 + 1)

            def sp(self, sp):
                sp.dma_start(self.G, self.gain.rearrange("(a d) -> a d", a=1).to_broadcast((128, D))).then_inc(n_gain_in, 16)

            def pool_store(self, pool):
                for t in range(NT):
                    pool.wait_ge(n_h_ready, self.at(t + 1, NT))
                    pool.dma_start(h_dram[t * 128:t * 128 + rows(t), :], self.HN[0:rows(t), t % 2, :]).then_inc(n_stored[t % 2], 16)
                for t in (NT - 2, NT - 1):
                    pool.wait_ge(n_stored[t % 2], self.at_store(t))

            def act(self, act, link):
                ss, ms = SM[:, 0:NT], SM[:, 8:8 + NT]
                for t in range(NT):
                    self.wait_x(act, t)
                    r = rows(t)
                    link(nc.scalar.activation(self.JUNK[0:r, :], X[0:r, t, :], ACT.Square, accum_out=ss[0:r, t:t + 1]))
                nc.scalar.activation(SM[:, 16:17], part[:, 0:1], ACT.Square).then_inc(n_squares, 1)
                act.wait_ge(n_means, self.at(1, 1))
                nc.scalar.activation(SM[:, 24:24 + NT], ms, ACT.Sqrt).then_inc(n_roots, 1)

            def act_copies(self, act):
                for t in range(TT):
                    for j in range(2):
                        act.wait_ge(n_turned, self.at(2 * t + j + 1, HALVES))
                        nc.scalar.activation(self.HT[:, 4 * j:4 * j + 4, t * 128:(t + 1) * 128],
                                             P[:, (2 * t + j) % 4, :].rearrange("p (k n) -> p k n", k=4), ACT.Copy).then_inc(n_copied, 1)
                act.wait_ge(n_turned, self.at(HALVES, HALVES))
                nc.scalar.activation(self.HT[:, :, NP_:TOK], P[:, 0, 0:KT * NS_].rearrange("p (k n) -> p k n", k=KT), ACT.Copy).then_inc(n_copied, 1)

            def dve(self, dve, link):
                ss, ms, rt, rr = SM[:, 0:NT], SM[:, 8:8 + NT], SM[:, 24:24 + NT], SM[:, 32:32 + NT]
                dve.wait_ge(n_squares, self.at(1, 1))
                nc.vector.tensor_scalar(ms, ss, 1.0 / D, EPS, ALU.mult, ALU.add).then_inc(n_means, 1)
                dve.wait_ge(n_roots, self.at(1, 1))
                link(nc.vector.reciprocal(rr, rt))
                dve.wait_ge(n_gain_in, self.at(16, 16))
                for t in range(NT):
                    r = rows(t)
                    if t >= 2:
                        dve.wait_ge(n_turned, self.at(2 * (t - 1), HALVES))
                        if self.store:
                            dve.wait_ge(n_stored[t % 2], self.at_store(t - 2))
                    nc.vector.scalar_tensor_tensor(out=self.HN[0:r, t % 2, :], in0=X[0:r, t, :], scalar=rr[0:r, t:t + 1],
                                                   in1=self.G[0:r, :], op0=ALU.mult, op1=ALU.mult).then_inc(n_h_ready, 1)

            def pe(self, pe):
                for t in range(TT):
                    pe.wait_ge(n_h_ready, self.at(t + 1, NT))
                    if t >= 2:
                        pe.wait_ge(n_copied, self.at(2 * (t - 1), HALVES))
                    for j in range(2):
                        for k in range(4):
                            last = nc.tensor.transpose(P[:, (2 * t + j) % 4, k * 128:(k + 1) * 128],
                                                       self.HN[:, t % 2, (4 * j + k) * 128:(4 * j + k + 1) * 128], ident)
                        last.then_inc(n_turned, 1)
                pe.wait_ge(n_h_ready, self.at(NT, NT))
                pe.wait_ge(n_copied, self.at(2 * TT - 2, HALVES))
                for k in range(KT):
                    last = nc.tensor.transpose(P[:, 0, k * NS_:(k + 1) * NS_], self.HN[0:NS_, TT % 2, k * 128:(k + 1) * 128], ident[0:NS_, 0:NS_])
                last.then_inc(n_turned, 1)



        WT = view(R, 0, KT, NCT)
        WN = view(R, KT * NCT, KT, NCN)
        WO = view(R, KT * (NCT + NCN), KT, D)
        M = {}

        def carve(t, at, **parts):
            for n, dims in parts.items():
                M[n] = view(t, at, *dims)
                at += int(np.prod(dims))
            return at

        end = carve(R, KT * (NCT + NCN + D), qa=(4, TOK), kdup=(AKV, TOK), qkp=(4, 3 + NP_), qks=(4, NS_, CONV),
                    vaug=(NT, BH, VA), mc=(mw,), va=(NT, 136), sink=(AH,))
        assert end <= 3 * EXP, (end, 3 * EXP)
        end = carve(AR, 0, ht=(KT, TOK), sog=(NT, 512), bias=(AH, 256), gain=(D,), wc=(4, CONV), bg=(8,), rel=(8,),
                    kout=(128,), kn=(8,), pm=(NS_, AH), sbias=(129,), sinkc=(1,))
        assert end <= 10240, end
        M["hn"] = view(AR, KT * TOK, 2, D)
        M["line"] = M["vaug"].rearrange("p a b c -> p (a b c)")[:, 0:384]
        M["cbuf"] = M["bias"].rearrange("p a b -> p (a b)")[:, 0:512]
        e1 = carve(R, 0, mix=(KT, TOK), lg=(2, 2, 256), pt=(2, 2, 128), kc=(NS_, 128), vc=(NS_, 128), scs=(NS_, 129),
                   kct=(2, 128), qb=(NS_, AH), pts=(NS_, AH))
        assert e1 <= KT * NCT, (e1, KT * NCT)
        e1b = carve(R, KT * TOK, hs=(TT, BH, DV))
        e1c = carve(R, KT * TOK, c0=(NS_, 2, VA), km=(2, 256), ew=(2, 32), hst=(32,), sq=(32,), wk=(2, 32), rc=(32,))
        assert max(e1b, e1c) <= KT * NCT
        e2 = carve(R, KT * NCT, qc=(4, TOK), sg=(TOK,), kw=(TT, 2, 64), dw=(2, 512), sw=(2, 512), cst=(2, VA), qs=(BH, 512), gmr=(512,),
                   cols=(2, TT, BH), dec=(2, TT), wv=(4, 16))
        assert e2 <= KT * (NCT + NCN), (e2 - KT * NCT, KT * NCN)
        M["sg4"] = view(R, KT * NCT + 4 * TOK, 4, TOK)
        carve(AR, 0, ig=(TOK,), fg=(TOK,), ab=(TOK,), lf=(TOK,), cum=(TOK,), gg=(TOK,), mm=(TOK,), em=(TOK,))

        names = """wqa_in wqk_in wva_in wg_in wv_in wog_in wo_in mc_in sink_in wc_in bg_in rel_in gmr_in cbuf_in rel_set line_made
                   line_out cv_out sinkc_in m_row line_stored bias_in cbuf_turned cbuf_copied pads_set ones_set projt projt_copied
                   projs projs_copied projn projn_copied kcache_in vcache_in scored shifted exped probs pt_turned pt_copied att
                   att_copied conv_sig conv_in conv_q qb_made sk_turned sk_copied s_scored s_logits s_exp s_probs s_pturned
                   s_pcopied s_pm s_att gates_made gates_turned lf_abs lf_log rows_g aw_made em_made cols_turned cols_copied bcast
                   qs_made dw_arg dw_exp st_done sw_made kt_turned kw_made upd_done st_new hs_ms hs_rt outb outb_turned
                   outb_copied kt_out kt_outc c0_in m0_in sm_row sm_exp sm_k sm_outer sm_c1 sm_h sm_ss sm_sqr sm_done sm_bc sm_w
                   sm_ms sm_qn sog_made sog_scaled sm_ex2 sm_km sm_out wout wout_added""".split()
        weight_in = {f"{n}{u}": sem(f"expert_{n}_in{u}") for n in ("gate", "up", "down") for u in range(3)}
        router_in = sem("router_in")
        act_links, dve_links = [0], [0]
        soft = [sem(f"pool_dma{i}") for i in range(SOFT)]
        lasting = [x for x in lasting if x not in soft]
        part_begins()
        by_pool = "rel_in cbuf_in sink_in wc_in sinkc_in bg_in line_stored bias_in gmr_in m0_in cv_out c0_in sm_out".split()
        E = {n: pool_sem() if n in by_pool else sem(n) for n in names}

        wi = A["w_in_mix"][0].rearrange("(k p) n -> p k n", p=128)

        def mixer_sp(sp):
            sp.dma_start(KC[:, :], A["keep"]).then_inc(keep_in, 16)
            for t in range(TT):
                sp.dma_start(X[:, t, :], A["x_prompt"][0, t * 128:(t + 1) * 128, :]).then_inc(x_in[t], 16)
            sp.dma_start(X[0:NS_, TT, :], A["x_sample"][:, 0, :]).then_inc(x_in[TT], 16)
            norm0.sp(sp)
            sp.dma_start(M["mc"], A["mixc"]).then_inc(E["mc_in"], 16)
            sp.dma_start(WT[:, :, 0:640], wi[:, :, 0:640]).then_inc(E["wqa_in"], 16)
            sp.dma_start(WT[:, :, 640:1152], wi[:, :, C_QK:C_V]).then_inc(E["wqk_in"], 16)
            sp.dma_start(WN[:, :, 0:128], wi[:, :, C_VA:C_QK]).then_inc(E["wva_in"], 16)
            sp.dma_start(WN[:, :, 128:136], wi[:, :, C_G:C_OG]).then_inc(E["wg_in"], 16)
            sp.dma_start(WN[:, :, 136:648], wi[:, :, C_V:C_G]).then_inc(E["wv_in"], 16)
            sp.dma_start(WN[:, :, 648:1160], wi[:, :, C_OG:C_OG + 512]).then_inc(E["wog_in"], 16)
            sp.dma_start(WO, A["w_out_mix"][0].rearrange("(k p) n -> p k n", p=128)).then_inc(E["wo_in"], 16)
            sp.wait_ge(E["projs"], 1)
            sp.dma_start(M["kc"], A["cache_win_k"][0].rearrange("b s j d -> s b (j d)")).then_inc(E["kcache_in"], 16)
            sp.dma_start(M["vc"], A["cache_win_v"][0].rearrange("b s j d -> s b (j d)")).then_inc(E["vcache_in"], 16)

        def out_dma(eng, dst, src):
            who, s = ("pool", out_pool) if eng is nc.gpsimd else ("sp", out_sp)
            eng.dma_start(dst, src).then_inc(s, 16)
            stores[who] += 16

        def mixer_pool(pool):
            pool.wait_ge(small_set, 1)
            pool.dma_start(M["rel"][0:32, :], A["rel_bias_table"]).then_inc(E["rel_in"], 16)
            pool.dma_start(M["cbuf"][0:24, :], A["state_mlstm_conv"][0].rearrange("b j c -> (b j) c")).then_inc(E["cbuf_in"], 16)
            pool.dma_start(M["sink"], A["attn_sinks"].to_broadcast((128, AH))).then_inc(E["sink_in"], 16)
            for c in range(4):
                pool.dma_start(M["wc"][:, c, :], A["w_mlstm_qk_conv"][0][:, c * 128:(c + 1) * 128].rearrange("j p -> p j")).then_inc(E["wc_in"], 16)
            pool.dma_start(M["sinkc"][0:AH, :], A["attn_sinks"].rearrange("a h -> h a")).then_inc(E["sinkc_in"], 16)
            pool.dma_start(M["bg"], A["b_mlstm_gates"].to_broadcast((128, 8))).then_inc(E["bg_in"], 16)
            pool.memset(M["qkp"][:, :, 0:CONV - 1], 0.0).then_inc(E["pads_set"], 1)
            pool.wait_ge(E["line_out"], 1)
            pool.dma_start(g_dram[:, 0:128 * 385].rearrange("h (q s) -> h q s", s=385)[:, :, 0:384],
                           M["line"][0:AH, :].unsqueeze(1).to_broadcast((AH, 128, 384))).then_inc(E["line_stored"], 16)
            pool.wait_ge(E["line_stored"], 16)
            pool.memset(M["vaug"][:, :, :, DV:VA], 1.0).then_inc(E["ones_set"], 1)
            pool.wait_ge(E["cbuf_turned"], 1)
            skew = g_dram[:, 127:127 + 128 * 384].rearrange("h (q s) -> q h s", s=384)
            pool.dma_start(M["bias"], skew[:, :, 0:256]).then_inc(E["bias_in"], 16)
            out_dma(pool, O["s_win_k"][0, :, 0:WIN - 1], A["cache_win_k"][0, :, 1:WIN])
            out_dma(pool, O["s_win_v"][0, :, 0:WIN - 1], A["cache_win_v"][0, :, 1:WIN])
            out_dma(pool, O["s_mlstm_conv"][0, :, 0:2, :], A["state_mlstm_conv"][0, :, 1:3, :])
            pool.wait_ge(E["projs"], 1)
            pool.memset(M["qb"], 0.0).then_inc(E["qb_made"], 1)
            pool.wait_ge(E["projn_copied"], NT)
            out_dma(pool, O["p_win_v"][0, 0].rearrange("s j d -> s (j d)"), M["va"][:, TT - 1, 0:128])
            out_dma(pool, O["s_win_v"][0, :, WIN - 1].rearrange("b j d -> b (j d)"), M["va"][0:NS_, TT, 0:128])
            pool.wait_ge(E["projn"], NT + len(GROUPS))
            pool.dma_start(M["gmr"], A["g_mlstm_norm"].to_broadcast((128, 512))).then_inc(E["gmr_in"], 16)
            pool.dma_start(SM[0:NS_, 64:68], A["state_mlstm_m"][0]).then_inc(E["m0_in"], 16)
            pool.wait_ge(E["gmr_in"], 16)
            pool.wait_ge(E["sog_made"], 1)
            for t in range(NT):
                q = slice(0, rows(t))
                nc.gpsimd.tensor_tensor(M["sog"][q, t, :], M["sog"][q, t, :], M["gmr"][q, :], ALU.mult).then_inc(E["sog_scaled"], 1)
            pool.wait_ge(E["kt_outc"], 1)
            out_dma(pool, O["p_win_k"][0, 0].rearrange("s j d -> s (j d)"), M["kout"])
            out_dma(pool, O["s_win_k"][0, :, WIN - 1].rearrange("b j d -> b (j d)"), M["sg"][0:NS_, 0:128])
            pool.dma_start(O["p_mlstm_conv"][0, 0], M["mix"][0:3, 4, 0:512]).then_inc(E["cv_out"], 16)
            pool.dma_start(O["s_mlstm_conv"][0, :, 2, :], M["mix"][0:NS_, 5, 0:512]).then_inc(E["cv_out"], 16)
            pool.wait_ge(E["m_row"], 1)
            out_dma(pool, O["p_mlstm_m"].rearrange("a b h -> h (a b)"), M["cum"][0:BH, NP_ - 1:NP_])
            for hp in range(2):
                pool.wait_ge(E["st_new"], TT * (hp + 1))
                out_dma(pool, O["p_mlstm_c"][0, 0, 2 * hp:2 * hp + 2].rearrange("h d v -> (h d) v"), M["cst"][:, hp, 0:DV])
                out_dma(pool, O["p_mlstm_n"][0, 0, 2 * hp:2 * hp + 2].rearrange("h (d a) -> (h d) a", a=1), M["cst"][:, hp, DV:VA])
            pool.wait_ge(E["outb_turned"], TT)
            for r in range(2):
                q = slice(r * 64, r * 64 + 64)
                pool.dma_start(M["c0"][q, :, :, 0:DV].rearrange("d b p v -> d (b p) v"), A["state_mlstm_c"][0].rearrange("b (p r) d v -> r d (b p) v", r=2)[r]).then_inc(E["c0_in"], 16)
                pool.dma_start(M["c0"][q, :, :, DV:VA].rearrange("d b p v -> d (b p) v"), A["state_mlstm_n"][0].rearrange("b (p r) (d v) -> r d (b p) v", r=2, v=1)[r]).then_inc(E["c0_in"], 16)
            pool.wait_ge(E["sm_row"], 2)
            out_dma(pool, O["s_mlstm_m"][0], SM[0:NS_, 84:88])
            pool.wait_ge(E["sm_c1"], NS_)
            for r in range(2):
                q = slice(r * 64, r * 64 + 64)
                pool.dma_start(O["s_mlstm_c"][0].rearrange("b (p r) d v -> r d (b p) v", r=2)[r], M["c0"][q, :, :, 0:DV].rearrange("d b p v -> d (b p) v")).then_inc(E["sm_out"], 16)
                pool.dma_start(O["s_mlstm_n"][0].rearrange("b (p r) (d v) -> r d (b p) v", r=2, v=1)[r], M["c0"][q, :, :, DV:VA].rearrange("d b p v -> d (b p) v")).then_inc(E["sm_out"], 16)
            pool.wait_ge(E["sm_out"], 64)
            pool.wait_ge(E["cv_out"], 32)

        STEPS = [(n, p) for n in range(TT) for p in range(AH // 2)]
        GROUPS = [(t, g) for t in range(NT) for g in (0, 1)]

        def mixer_pe(pe):
            cat = lambda n: M["mc"][:, mlay[n][0]:mlay[n][0] + mlay[n][1]]
            pe.wait_ge(E["mc_in"], 16)
            pe.wait_ge(E["rel_in"], 16)
            pe.wait_ge(E["rel_set"], 1)
            nc.tensor.matmul(P[0:AH, 7, 0:384], M["rel"][0:33, :], cat("bucket")[0:33, :], start=True, stop=True).then_inc(E["line_made"], 1)
            pe.wait_ge(keep_in, 16)
            pe.wait_ge(E["cbuf_in"], 16)
            for c in range(4):
                last = nc.tensor.transpose(P[:, 6, 128 + c * 24:152 + c * 24], M["cbuf"][0:24, c * 128:(c + 1) * 128], ident[0:24, 0:24])
            last.then_inc(E["cbuf_turned"], 1)
            norm0.pe(pe)
            pe.wait_ge(n_copied, HALVES)
            pe.wait_ge(E["cbuf_copied"], 1)
            HT = M["ht"]
            for m in range(9):
                if m == 0:
                    pe.wait_ge(E["wqa_in"], 16)
                if m == 5:
                    pe.wait_ge(E["wqk_in"], 16)
                if m >= 2:
                    pe.wait_ge(E["projt_copied"], m - 1)
                for k in range(KT):
                    last = nc.tensor.matmul(P[:, 4 + m % 2, :], WT[:, k, m * 128:(m + 1) * 128], HT[:, k, 0:NP_], start=(k == 0), stop=(k == KT - 1))
                last.then_inc(E["projt"], 1)
                for k in range(KT):
                    last = nc.tensor.matmul(P[:, 6, m * NS_:(m + 1) * NS_], WT[:, k, m * 128:(m + 1) * 128], HT[:, k, NP_:TOK], start=(k == 0), stop=(k == KT - 1))
            last.then_inc(E["projs"], 1)

            def by_token(g, t, lo, hi):
                if g >= 4:
                    pe.wait_ge(E["projn_copied"], g - 3)
                r = rows(t)
                for k in range(KT):
                    last = nc.tensor.matmul(P[0:r, g % 4, 0:hi - lo], HT[:, k, t * 128:t * 128 + r], WN[:, k, lo:hi], start=(k == 0), stop=(k == KT - 1))
                last.then_inc(E["projn"], 1)

            pe.wait_ge(E["wva_in"], 16)
            pe.wait_ge(E["wg_in"], 16)
            for t in range(NT):
                by_token(t, t, 0, 136)
            pe.wait_ge(E["wv_in"], 16)
            pe.wait_ge(E["wog_in"], 16)
            pe.wait_ge(E["projt_copied"], 9)
            pe.wait_ge(E["projs_copied"], 1)
            qa, kd, va = M["qa"], M["kdup"], M["va"]

            def score(i):
                n, p = STEPS[i]
                lo = max(n - 1, 0) * 128
                if i:
                    pe.wait_ge(E["shifted"], i)
                for r in range(2):
                    q = slice(r * 64, r * 64 + 64)
                    last = nc.tensor.matmul(P[:, 4 + r, lo + 128 - n * 128:256], qa[q, p, n * 128:(n + 1) * 128], kd[q, p // 2, lo:(n + 1) * 128], start=True, stop=True)
                last.then_inc(E["scored"], 1)

            def turn(i):
                n, p = STEPS[i]
                pe.wait_ge(E["probs"], i + 1)
                if i:
                    pe.wait_ge(E["pt_copied"], i)
                for r in range(2):
                    for j in range(0 if n else 1, 2):
                        last = nc.tensor.transpose(P[:, 6, (2 * r + j) * 128:(2 * r + j + 1) * 128], M["lg"][:, i % 2, r, j * 128:(j + 1) * 128], ident)
                last.then_inc(E["pt_turned"], 1)

            def attend(i):
                n, p = STEPS[i]
                kv = p // 2
                pe.wait_ge(E["pt_copied"], i + 1)
                if i:
                    pe.wait_ge(E["att_copied"], i)
                for r in range(2):
                    for j in range(0 if n else 1, 2):
                        last = nc.tensor.matmul(P[r * 64:r * 64 + 64, 7, 0:128], va[:, n - 1 + j, kv * 64:kv * 64 + 64], M["pt"][:, r, j, :],
                                                start=(j == 0 or n == 0), stop=(j == 1))
                last.then_inc(E["att"], 1)

            for i in range(len(STEPS) + 1):
                if i < len(STEPS):
                    score(i)
                if i:
                    turn(i - 1)
                if i < len(GROUPS):
                    t, g = GROUPS[i]
                    by_token(NT + i, t, 136 + 512 * g, 648 + 512 * g)
                if i:
                    attend(i - 1)

            pe.wait_ge(E["kcache_in"], 16)
            pe.wait_ge(E["qb_made"], 2)
            pe.wait_ge(E["projn_copied"], NT + len(GROUPS))
            pe.wait_ge(E["att_copied"], len(STEPS))
            for b in range(NS_):
                if b >= 2:
                    pe.wait_ge(E["sk_copied"], b - 1)
                nc.tensor.transpose(P[:, b % 2, 0:128], M["kc"][:, b, :], ident).then_inc(E["sk_turned"], 1)
                if b >= 1:
                    sample_score(pe, b - 1)
            sample_score(pe, NS_ - 1)
            pe.wait_ge(E["s_probs"], 1)
            for b in range(NS_):
                last = nc.tensor.transpose(P[:, 4, b * AH:(b + 1) * AH], M["scs"][0:AH, b, 0:128], ident[0:AH, 0:AH])
            nc.tensor.transpose(P[0:NS_, 5, 0:AH], M["scs"][0:AH, :, 128], ident[0:AH, 0:AH]).then_inc(E["s_pturned"], 1)
            pe.wait_ge(E["s_pcopied"], 1)
            pe.wait_ge(E["s_pm"], 1)
            pe.wait_ge(E["vcache_in"], 16)
            for b in range(NS_):
                nc.tensor.matmul(P[:, 6, b * AH:(b + 1) * AH], M["vc"][:, b, :], M["pts"][:, b, :], start=True, stop=False)
                last = nc.tensor.matmul(P[:, 6, b * AH:(b + 1) * AH], va[0:NS_, TT, 0:128], M["pm"][0:NS_, b, :], start=False, stop=True)
            last.then_inc(E["s_att"], 1)
            for j in range(AKV):
                nc.tensor.transpose(P[:, 7, j * 64:j * 64 + 64], kd[0:64, j, NP_ - 128:NP_], ident[0:64, 0:64])
            nc.tensor.transpose(P[0:NS_, 7, 128:256], M["kn"], ident)
            for c in range(4):
                nc.tensor.transpose(P[0:3, 2, c * 128:(c + 1) * 128], M["qkp"][:, c, NP_:NP_ + 3], ident)
                last = nc.tensor.transpose(P[0:NS_, 3, c * 128:(c + 1) * 128], M["qks"][:, c, :, 3], ident)
            last.then_inc(E["kt_out"], 1)

            pe.wait_ge(E["gates_made"], 1)
            pe.wait_ge(E["kt_outc"], 1)
            for w, bank in ((0, 0), (1, 1)):
                for t in range(TT):
                    last = nc.tensor.transpose(P[0:BH, bank, t * 128:(t + 1) * 128], va[:, t, 128 + 4 * w:132 + 4 * w], ident)
            last.then_inc(E["gates_turned"], 1)
            pe.wait_ge(E["rows_g"], 1)
            pe.wait_ge(E["em_made"], 1)
            pe.wait_ge(E["aw_made"], 1)
            for t in range(TT):
                nc.tensor.transpose(P[:, 2, t * 4:t * 4 + 4], M["gg"][0:BH, t * 128:(t + 1) * 128], ident[0:BH, 0:BH])
                last = nc.tensor.transpose(P[:, 2, 16 + t * 4:20 + t * 4], M["em"][0:BH, t * 128:(t + 1) * 128], ident[0:BH, 0:BH])
            last.then_inc(E["cols_turned"], 1)
            pe.wait_ge(E["cols_copied"], 1)
            for h in range(BH):
                nc.tensor.matmul(P[:, h, :], cat("sel")[0:BH, h * 128:(h + 1) * 128], M["mm"][0:BH, 0:NP_], start=True, stop=True)
                nc.tensor.matmul(P[:, 4 + h, :], cat("half")[0:BH, h * 128:(h + 1) * 128], M["ab"][0:BH, 0:NP_], start=True, stop=True).then_inc(E["bcast"], 1)
            qc = M["qc"]
            pe.wait_ge(E["conv_q"], 1)
            for hp in range(2):
                pe.wait_ge(E["qs_made"], 2 * hp + 2)
                for r in range(2):
                    h, q = 2 * hp + r, slice(r * 64, r * 64 + 64)
                    for c in range(TT):
                        cs = slice(c * 128, (c + 1) * 128)
                        last = nc.tensor.matmul(P[:, 4 + h, cs], qc[q, 2 + hp, cs], qc[q, hp, cs], start=True, stop=True)
                    last.then_inc(E["st_done"], 1)
                pe.wait_ge(E["dw_arg"], 2 * hp + 2)
                for c in range(TT):
                    last = nc.tensor.transpose(P[:, 2 * hp, c * 128:(c + 1) * 128], qc[:, 2 + hp, c * 128:(c + 1) * 128], ident)
                last.then_inc(E["kt_turned"], 1)
                pe.wait_ge(E["sw_made"], 2 * hp + 2)
                pe.wait_ge(E["kw_made"], hp + 1)
                for c in range(TT):
                    u = TT * hp + c
                    cs = slice(c * 128, (c + 1) * 128)
                    if c:
                        pe.wait_ge(E["st_new"], u)
                    for r in range(2):
                        h = 2 * hp + r
                        last = nc.tensor.matmul(P[:, 2 * hp + 1, r * VA:(r + 1) * VA], M["sw"][:, r, cs], M["vaug"][:, c, h, :], start=True, stop=(c == 0))
                        if c:
                            last = nc.tensor.matmul(P[:, 2 * hp + 1, r * VA:(r + 1) * VA], M["qs"][:, h, cs], M["cst"][:, hp, :], start=False, stop=True)
                    last
                    for r in range(2):
                        h = 2 * hp + r
                        last = nc.tensor.matmul(P[r * 64:r * 64 + 64, 4 + 2 * hp, 0:VA], M["kw"][:, c, r, :], M["vaug"][:, c, h, :], start=True, stop=True)
                    last.then_inc(E["upd_done"], 1)
            pe.wait_ge(E["outb"], 1)
            for t in range(TT):
                for h in range(BH):
                    last = nc.tensor.transpose(P[:, t, h * 128:(h + 1) * 128], M["hs"][:, t, h, :], ident)
                last.then_inc(E["outb_turned"], 1)

            pe.wait_ge(E["outb_copied"], TT)
            pe.wait_ge(E["sog_scaled"], NT)
            for hp in range(2):
                last = nc.tensor.transpose(P[0:NS_, 0, hp * 128:(hp + 1) * 128], qc[:, 2 + hp, NP_:TOK], ident)
            for h in range(BH):
                last = nc.tensor.transpose(P[:, 0, 256 + h * 8:264 + h * 8], M["sog"][0:NS_, TT, h * 128:(h + 1) * 128], ident[0:NS_, 0:NS_])
            last.then_inc(E["sm_k"], 1)
            pe.wait_ge(E["wo_in"], 16)

            def out_project(*groups):
                for g in groups:
                    t, hf, r = g // 2, g % 2, rows(g // 2)
                    if g >= 4:
                        pe.wait_ge(E["wout_added"], g - 3)
                    for k in range(KT):
                        last = nc.tensor.matmul(P[0:r, 4 + g % 4, :], M["mix"][:, k, t * 128:t * 128 + r], WO[:, k, hf * 512:(hf + 1) * 512], start=(k == 0), stop=(k == KT - 1))
                    last.then_inc(E["wout"], 1)

            def outer(*samples):
                for b in samples:
                    pe.wait_ge(E["sm_km"], b + 1)
                    if b >= 2:
                        pe.wait_ge(E["sm_c1"], b - 1)
                    for h in range(BH):
                        r, hp = h % 2, h // 2
                        last = nc.tensor.matmul(P[r * 64:r * 64 + 64, 1 + b % 2, hp * VA:(hp + 1) * VA], M["km"][0:NS_, b % 2, h * 64:(h + 1) * 64],
                                                M["vaug"][0:NS_, TT, h, :], start=True, stop=True)
                    last.then_inc(E["sm_outer"], 1)

            out_project(0)
            pe.wait_ge(E["sm_w"], 1)
            nc.tensor.matmul(P[:, 3, 0:64], ones[0:NS_, :], M["ew"].rearrange("p a b -> p (a b)")[0:NS_, :], start=True, stop=True).then_inc(E["sm_bc"], 1)
            out_project(1)
            outer(0, 1)
            out_project(2)
            outer(2, 3)
            out_project(3)
            outer(4, 5)
            out_project(4)
            outer(6, 7)
            out_project(5)
            pe.wait_ge(E["sm_c1"], NS_)
            pe.wait_ge(E["sm_qn"], 1)
            for r in range(2):
                q = slice(r * 64, r * 64 + 64)
                for b in range(NS_):
                    for hp in range(2):
                        j = b * BH + 2 * hp + r
                        nc.tensor.matmul(P[:, 1 + r, j:j + 1], M["c0"][q, b, hp, 0:DV], qc[q, hp, NP_ + b:NP_ + b + 1], start=True, stop=True)
                last = nc.tensor.matmul(P[:, 1 + r, 64:80], ones[q, :], M["hst"][q, 0:16], start=True, stop=True)
            last.then_inc(E["sm_h"], 1)
            out_project(6)
            pe.wait_ge(E["sm_sqr"], 1)
            nc.tensor.matmul(P[:, 3, 64:96], ones, M["sq"], start=True, stop=True).then_inc(E["sm_ss"], 1)
            out_project(7)
            pe.wait_ge(E["sm_done"], 1)
            out_project(8, 9)

        def sample_score(pe, b):
            pe.wait_ge(E["sk_copied"], b + 1)
            if b >= 2:
                pe.wait_ge(E["s_logits"], b - 1)
            nc.tensor.matmul(P[0:AH, 2 + b % 2, 0:128], M["qb"][:, b, :], M["kct"][:, b % 2, :], start=True, stop=True)
            nc.tensor.matmul(P[0:AH, 2 + b % 2, 128:129], M["qb"][:, b, :], M["kn"][:, b:b + 1], start=True, stop=True).then_inc(E["s_scored"], 1)

        def mixer_act(act):
            link = Chain(act, act_seq)
            act.wait_ge(keep_in, 16)
            act.wait_ge(small_set, 1)
            norm0.act(act, link)
            norm0.act_copies(act)
            cp = lambda o, i: nc.scalar.activation(o, i, ACT.Copy)
            qa, kd = M["qa"], M["kdup"]
            for m in range(9):
                act.wait_ge(E["projt"], m + 1)
                b = P[:, 4 + m % 2, :]
                if m < 4:
                    last = cp(qa[:, m, 0:NP_], b)
                elif m == 4:
                    for j in range(AKV):
                        for q in range(2):
                            last = cp(kd[q * 64:q * 64 + 64, j, 0:NP_], P[j * 64:j * 64 + 64, 4, :])
                else:
                    last = cp(M["qkp"][:, m - 5, 3:3 + NP_], b)
                last.then_inc(E["projt_copied"], 1)
            act.wait_ge(E["projs"], 1)
            s6 = P[:, 6, 0:72].rearrange("p (m b) -> p m b", m=9)
            cp(qa[:, :, NP_:TOK], s6[:, 0:4, :])
            for j in range(AKV):
                for q in range(2):
                    cp(kd[q * 64:q * 64 + 64, j, NP_:TOK], P[j * 64:j * 64 + 64, 6, 32:40])
            cp(M["kn"], P[:, 6, 32:40])
            cp(M["qks"][:, :, :, 3], s6[:, 5:9, :]).then_inc(E["projs_copied"], 1)
            for t in range(NT):
                act.wait_ge(E["projn"], t + 1)
                cp(M["va"][0:rows(t), t, :], P[0:rows(t), t % 4, 0:136]).then_inc(E["projn_copied"], 1)
            act.wait_ge(E["ones_set"], 1)

            def pt_copy(i):
                act.wait_ge(E["pt_turned"], i + 1)
                if i:
                    act.wait_ge(E["att"], i)
                j = 0 if STEPS[i][0] else 1
                cp(M["pt"][:, :, j:2, :], P[:, 6, :].rearrange("p (r j n) -> p r j n", r=2, j=2)[:, :, j:2, :]).then_inc(E["pt_copied"], 1)

            for i, (n, p) in enumerate(STEPS):
                lo = 0 if n else 128
                act.wait_ge(E["shifted"], i + 1)
                L = M["lg"][:, i % 2, :, lo:256]
                st = SM[:, 96 + 8 * (i % 2):104 + 8 * (i % 2)]
                for r in range(2):
                    nc.scalar.activation(L[:, r, :], L[:, r, :], ACT.Exp, bias=st[:, r:r + 1], accum_out=st[:, 4 + r:5 + r])
                nc.scalar.activation(st[:, 6:8], st[:, 2:4], ACT.Exp).then_inc(E["exped"], 1)
                if i:
                    pt_copy(i - 1)
                if i < len(GROUPS):
                    t, g = GROUPS[i]
                    act.wait_ge(E["projn"], NT + i + 1)
                    b, r = P[0:rows(t), (NT + i) % 4, :], rows(t)
                    if g == 0:
                        cp(M["vaug"][0:r, t, :, 0:DV], b.rearrange("p (h v) -> p h v", h=BH)).then_inc(E["projn_copied"], 1)
                    else:
                        cp(M["sog"][0:r, t, :], b).then_inc(E["projn_copied"], 1)
            pt_copy(len(STEPS) - 1)
            act.wait_ge(E["conv_in"], 4)
            nc.scalar.activation(M["sg4"], M["qc"], ACT.Sigmoid).then_inc(E["conv_sig"], 1)
            for v in (M["sog"][:, 0:TT, :], M["sog"][0:NS_, TT, :]):
                last = nc.scalar.activation(v, v, ACT.Sigmoid)
            last.then_inc(E["sog_made"], 1)
            for b in range(NS_):
                act.wait_ge(E["sk_turned"], b + 1)
                if b >= 2:
                    act.wait_ge(E["s_scored"], b - 1)
                cp(M["kct"][:, b % 2, :], P[:, b % 2, 0:128]).then_inc(E["sk_copied"], 1)
            act.wait_ge(E["s_exp"], 1)
            nc.scalar.activation(M["scs"][0:AH], M["scs"][0:AH], ACT.Exp)
            nc.scalar.activation(SM[0:AH, 128:136], SM[0:AH, 128:136], ACT.Exp).then_inc(E["s_exp"], 1)
            act.wait_ge(E["lf_abs"], 1)
            link(nc.scalar.activation(M["ab"][0:BH, 0:NP_], M["ab"][0:BH, 0:NP_], ACT.Exp, scale=-1.0))
            nc.scalar.activation(M["ab"][0:BH, 0:NP_], M["ab"][0:BH, 0:NP_], ACT.Ln, bias=1.0).then_inc(E["lf_log"], 1)
            act.wait_ge(E["m_row"], 1)
            nc.scalar.activation(M["em"][0:BH, 0:NP_], M["cum"][0:BH, 0:NP_], ACT.Exp, scale=-1.0).then_inc(E["em_made"], 1)
            for c in range(TT):
                cs = slice(c * 128, (c + 1) * 128)
                last = nc.scalar.activation(M["ab"][0:BH, cs], M["mm"][0:BH, cs], ACT.Exp, scale=-1.0, bias=SM[0:BH, 40 + c:41 + c])
            last.then_inc(E["aw_made"], 1)
            for h in range(BH):
                act.wait_ge(E["dw_arg"], h + 1)
                nc.scalar.activation(M["dw"][:, h % 2, :], M["dw"][:, h % 2, :], ACT.Exp, scale=-1.0).then_inc(E["dw_exp"], 1)
            act.wait_ge(E["hs_ms"], 1)
            nc.scalar.activation(SM[:, 160:176], SM[:, 160:176], ACT.Sqrt).then_inc(E["hs_rt"], 1)
            act.wait_ge(E["cv_out"], 32)
            for t in range(TT):
                act.wait_ge(E["outb_turned"], t + 1)
                cp(M["mix"][:, 4:8, t * 128:(t + 1) * 128], P[:, t, :].rearrange("p (h n) -> p h n", h=4)).then_inc(E["outb_copied"], 1)
            act.wait_ge(E["sm_row"], 1)
            link(nc.scalar.activation(SM[0:NS_, 68:72], SM[0:NS_, 68:72], ACT.Exp, scale=-1.0))
            nc.scalar.activation(SM[0:NS_, 68:72], SM[0:NS_, 68:72], ACT.Ln, bias=1.0).then_inc(E["sm_exp"], 1)
            act.wait_ge(E["sm_row"], 2)
            nc.scalar.activation(SM[0:NS_, 72:84], SM[0:NS_, 72:84], ACT.Exp).then_inc(E["sm_exp"], 1)
            act.wait_ge(E["sm_ms"], 1)
            nc.scalar.activation(M["sq"], M["sq"], ACT.Sqrt).then_inc(E["sm_ex2"], 1)
            return link.n

        def mixer_dve(dve):
            link = Chain(dve, dve_seq)
            V = nc.vector
            V.memset(SM[:, :], 0.0).then_inc(small_set, 1)
            V.memset(M["rel"][32:33, :], -BIG).then_inc(E["rel_set"], 1)
            dve.wait_ge(E["line_made"], 1)
            link(V.tensor_copy(M["line"][0:AH, :], P[0:AH, 7, 0:384]))
            V.tensor_copy(M["sbias"][0:AH, :], M["line"][0:AH, 127:256]).then_inc(E["line_out"], 1)
            norm0.dve(dve, link)
            dve.wait_ge(E["cbuf_turned"], 1)
            for c in range(4):
                last = V.tensor_copy(M["qks"][:, c, :, 0:3], P[:, 6, 128 + c * 24:152 + c * 24].rearrange("p (b j) -> p b j", j=3))
            last.then_inc(E["cbuf_copied"], 1)
            va, sk, sog = M["va"], M["sink"], M["sog"]
            dve.wait_ge(E["bg_in"], 16)
            dve.wait_ge(E["projn_copied"], NT)
            V.tensor_tensor(va[:, 0:TT, 128:136], va[:, 0:TT, 128:136], M["bg"].unsqueeze(1).to_broadcast((128, TT, 8)), ALU.add)
            V.tensor_tensor(va[0:NS_, TT, 128:136], va[0:NS_, TT, 128:136], M["bg"][0:NS_, :], ALU.add).then_inc(E["gates_made"], 1)
            dve.wait_ge(E["sink_in"], 16)
            dve.wait_ge(E["bias_in"], 16)

            def att_copy(i):
                n, p = STEPS[i]
                dve.wait_ge(E["att"], i + 1)
                V.tensor_copy(M["mix"][:, p, n * 128:(n + 1) * 128], P[:, 7, 0:128]).then_inc(E["att_copied"], 1)

            def conv(c):
                if c == 0:
                    dve.wait_ge(E["pads_set"], 1)
                    dve.wait_ge(E["wc_in"], 64)
                    dve.wait_ge(E["projs_copied"], 1)
                    dve.wait_ge(E["projn"], NT + len(GROUPS))
                w, qc = M["wc"], M["qc"]
                for lo, hi, src in ((0, NP_, lambda j: M["qkp"][:, c, j:j + NP_]), (NP_, TOK, lambda j: M["qks"][:, c, :, j])):
                    link(V.tensor_scalar(qc[:, c, lo:hi], src(0), w[:, c, 0:1], None, ALU.mult))
                    for j in range(1, CONV):
                        ins = V.scalar_tensor_tensor(out=qc[:, c, lo:hi], in0=src(j), scalar=w[:, c, j:j + 1], in1=qc[:, c, lo:hi], op0=ALU.mult, op1=ALU.add)
                        if j < CONV - 1 or hi == NP_:
                            link(ins)
                ins.then_inc(E["conv_in"], 1)

            def step(i):
                n, p = STEPS[i]
                lo = 0 if n else 128
                return p, lo, M["lg"][:, i % 2, :, lo:256], SM[:, 96 + 8 * (i % 2):104 + 8 * (i % 2)]

            def logits(i):
                p, lo, L, st = step(i)
                dve.wait_ge(E["scored"], i + 1)
                if i >= 2:
                    dve.wait_ge(E["pt_turned"], i - 1)
                link(V.scalar_tensor_tensor(out=L, in0=P[:, 4:6, lo:256], scalar=HD ** -0.5, in1=M["bias"][:, 2 * p:2 * p + 2, lo:256], op0=ALU.mult, op1=ALU.add))
                link(V.tensor_reduce(st[:, 0:2], L, AX, ALU.max))
                link(V.tensor_tensor(st[:, 2:4], st[:, 0:2], sk[:, 2 * p:2 * p + 2], ALU.max))
                link(V.tensor_scalar(st[:, 0:2], st[:, 2:4], -1.0, None, ALU.mult))
                V.tensor_tensor(st[:, 2:4], sk[:, 2 * p:2 * p + 2], st[:, 0:2], ALU.add).then_inc(E["shifted"], 1)

            logits(0)
            for i in range(len(STEPS)):
                ahead = i >= len(GROUPS)
                if ahead and i + 1 < len(STEPS):
                    logits(i + 1)
                p, lo, L, st = step(i)
                dve.wait_ge(E["exped"], i + 1)
                link(V.tensor_tensor(st[:, 4:6], st[:, 4:6], st[:, 6:8], ALU.add))
                link(V.reciprocal(st[:, 4:6], st[:, 4:6]))
                V.tensor_tensor(L, L, st[:, 4:6].unsqueeze(2).to_broadcast((128, 2, 256 - lo)), ALU.mult).then_inc(E["probs"], 1)
                if i:
                    att_copy(i - 1)
                if not ahead:
                    logits(i + 1)
                if i in CONV_AT:
                    conv(CONV_AT.index(i))
            att_copy(len(STEPS) - 1)
            dve.wait_ge(E["conv_sig"], 1)
            V.tensor_tensor(M["qc"][:, 0:2, :], M["qc"][:, 0:2, :], M["sg4"][:, 0:2, :], ALU.mult)
            V.scalar_tensor_tensor(out=M["qc"][:, 2:4, :], in0=M["qc"][:, 2:4, :], scalar=DK ** -0.5, in1=M["sg4"][:, 2:4, :], op0=ALU.mult, op1=ALU.mult).then_inc(E["conv_q"], 1)

            dve.wait_ge(E["qb_made"], 1)
            qv = M["qa"][:, :, NP_:TOK]
            for kv in range(AKV):
                for r in range(2):
                    last = V.tensor_copy(M["qb"][kv * 64:kv * 64 + 64, :, :].rearrange("p b (i r) -> p i r b", r=2)[:, 2 * kv:2 * kv + 2, r, :],
                                         qv[r * 64:r * 64 + 64, 2 * kv:2 * kv + 2, :])
            last.then_inc(E["qb_made"], 1)
            sc = M["scs"]
            for b in range(NS_):
                dve.wait_ge(E["s_scored"], b + 1)
                V.scalar_tensor_tensor(out=sc[0:AH, b, :], in0=P[0:AH, 2 + b % 2, 0:129], scalar=HD ** -0.5, in1=M["sbias"][0:AH, :],
                                       op0=ALU.mult, op1=ALU.add).then_inc(E["s_logits"], 1)
            dve.wait_ge(E["s_logits"], NS_)
            dve.wait_ge(E["sinkc_in"], 16)
            mx, es, su = SM[0:AH, 120:128], SM[0:AH, 128:136], SM[0:AH, 136:144]
            link(V.tensor_reduce(mx, sc[0:AH], AX, ALU.max))
            link(V.tensor_scalar(mx, mx, M["sinkc"][0:AH, :], None, ALU.max))
            V.tensor_scalar(es, mx, -1.0, M["sinkc"][0:AH, :], ALU.mult, ALU.add)
            V.tensor_tensor(sc[0:AH], sc[0:AH], mx.unsqueeze(2).to_broadcast((AH, NS_, 129)), ALU.subtract).then_inc(E["s_exp"], 1)
            dve.wait_ge(E["s_exp"], 2)
            link(V.tensor_reduce(su, sc[0:AH], AX, ALU.add))
            link(V.tensor_tensor(su, su, es, ALU.add))
            link(V.reciprocal(su, su))
            V.tensor_tensor(sc[0:AH], sc[0:AH], su.unsqueeze(2).to_broadcast((AH, NS_, 129)), ALU.mult).then_inc(E["s_probs"], 1)
            dve.wait_ge(E["s_pturned"], 1)
            V.tensor_copy(M["pts"], P[:, 4, 0:64].rearrange("p (b h) -> p b h", h=AH)).then_inc(E["s_pcopied"], 1)
            V.tensor_tensor(M["pm"][0:NS_], P[0:NS_, 5, 0:AH].unsqueeze(1).to_broadcast((NS_, NS_, AH)),
                            ident[0:NS_, 0:NS_].unsqueeze(2).to_broadcast((NS_, NS_, AH)), ALU.mult).then_inc(E["s_pm"], 1)
            dve.wait_ge(E["s_att"], 1)
            a6 = P[:, 6, 0:64].rearrange("p (b i r) -> p i r b", b=NS_, r=2)
            for kv in range(AKV):
                for r in range(2):
                    V.tensor_copy(M["mix"][r * 64:r * 64 + 64, 2 * kv:2 * kv + 2, NP_:TOK], a6[kv * 64:kv * 64 + 64, 2 * kv:2 * kv + 2, r, :])
            dve.wait_ge(E["kt_out"], 1)
            dve.wait_ge(E["conv_q"], 1)
            V.tensor_copy(M["kout"], P[:, 7, 0:128])
            V.tensor_copy(M["sg"][0:NS_, 0:128], P[0:NS_, 7, 128:256])
            V.tensor_copy(M["mix"][0:3, 4, 0:512], P[0:3, 2, :])
            V.tensor_copy(M["mix"][0:NS_, 5, 0:512], P[0:NS_, 3, :]).then_inc(E["kt_outc"], 1)

            row = lambda n: M[n][0:BH, 0:NP_]
            dve.wait_ge(E["gates_turned"], 1)
            link(V.tensor_copy(row("fg"), P[0:BH, 1, :]))
            V.scalar_tensor_tensor(out=row("ab"), in0=row("fg"), scalar=-1.0, in1=row("fg"), op0=ALU.mult, op1=ALU.max).then_inc(E["lf_abs"], 1)
            V.tensor_copy(row("ig"), P[0:BH, 0, :])
            link(V.memset(row("em"), 0.0))
            V.memset(SM[0:BH, 40:41], -BIG)
            dve.wait_ge(E["lf_log"], 1)
            link(V.scalar_tensor_tensor(out=row("lf"), in0=row("fg"), scalar=0.0, in1=row("ab"), op0=ALU.min, op1=ALU.subtract))
            for c in range(TT):
                cs = slice(c * 128, (c + 1) * 128)
                ins = V.tensor_tensor_scan(M["cum"][0:BH, cs], M["lf"][0:BH, cs], M["em"][0:BH, cs], 0.0, ALU.add, ALU.add)
            link(ins)
            link(V.tensor_tensor(row("gg"), row("ig"), row("cum"), ALU.subtract))
            for c in range(TT):
                cs, e = slice(c * 128, (c + 1) * 128), (c + 1) * 128
                link(V.tensor_tensor_scan(M["mm"][0:BH, cs], M["gg"][0:BH, cs], M["gg"][0:BH, cs], SM[0:BH, 40 + c:41 + c], ALU.max, ALU.max))
                if c < TT - 1:
                    link(V.tensor_tensor(SM[0:BH, 41 + c:42 + c], M["mm"][0:BH, e - 1:e], M["cum"][0:BH, e - 1:e], ALU.add))
            V.memset(SM[0:BH, 46:47], 0.0).then_inc(E["rows_g"], 1)
            V.tensor_tensor(row("cum"), row("cum"), row("mm"), ALU.add).then_inc(E["m_row"], 1)
            dve.wait_ge(E["cols_turned"], 1)
            V.tensor_copy(M["cols"].rearrange("p a t h -> p (a t h)"), P[:, 2, 0:32]).then_inc(E["cols_copied"], 1)
            late = M["mc"][:, mlay["late"][0]:mlay["late"][0] + 128]
            qc, dw, sw, dec = M["qc"], M["dw"], M["sw"], M["dec"]
            for h in range(BH):
                q = slice(h % 2 * 64, h % 2 * 64 + 64)
                dve.wait_ge(E["bcast"], h + 1)
                V.tensor_copy(dec[q, h // 2, :], P[q, 4 + h, 127:512:128])
                V.tensor_tensor(M["qs"][:, h, :], qc[:, h // 2, 0:NP_], P[:, 4 + h, :], ALU.mult).then_inc(E["qs_made"], 1)
            dve.wait_ge(E["cols_copied"], 1)
            for hp in range(2):
                for r in range(2):
                    h = 2 * hp + r
                    for c in range(TT):
                        cs = slice(c * 128, (c + 1) * 128)
                        last = V.scalar_tensor_tensor(out=dw[:, r, cs], in0=P[:, h, cs], scalar=M["cols"][:, 0, c, h:h + 1], in1=late, op0=ALU.subtract, op1=ALU.max)
                    last.then_inc(E["dw_arg"], 1)
                for r in range(2):
                    h = 2 * hp + r
                    dve.wait_ge(E["dw_exp"], h + 1)
                    dve.wait_ge(E["st_done"], h + 1)
                    V.tensor_tensor(sw[:, r, :], P[:, 4 + h, :], dw[:, r, :], ALU.mult).then_inc(E["sw_made"], 1)
                dve.wait_ge(E["kt_turned"], hp + 1)
                for r in range(2):
                    for c in range(TT):
                        last = V.tensor_scalar(M["kw"][:, c, r, :], P[:, 2 * hp, c * 128 + r * 64:c * 128 + r * 64 + 64], dw[:, r, c * 128 + 127:c * 128 + 128], None, ALU.mult)
                last.then_inc(E["kw_made"], 1)
                for c in range(TT):
                    u = TT * hp + c
                    dve.wait_ge(E["upd_done"], u + 1)
                    C = M["cst"][:, hp, :]
                    if c == 0:
                        V.tensor_copy(C, P[:, 4 + 2 * hp, 0:VA])
                    else:
                        dve.wait_ge(E["st_new"], u)
                        V.scalar_tensor_tensor(out=C, in0=C, scalar=dec[:, hp, c:c + 1], in1=P[:, 4 + 2 * hp, 0:VA], op0=ALU.mult, op1=ALU.add)
                    wv = M["wv"][:, c, 4 * hp:4 * hp + 4]
                    den = P[:, 2 * hp + 1, DV:DV + VA + 1:VA]
                    emc = M["cols"][:, 1, c, 2 * hp:2 * hp + 2]
                    V.tensor_tensor(wv[:, 0:2], den, emc, ALU.max)
                    link(V.scalar_tensor_tensor(out=wv[:, 2:4], in0=den, scalar=-1.0, in1=emc, op0=ALU.mult, op1=ALU.max))
                    link(V.tensor_tensor(wv[:, 2:4], wv[:, 0:2], wv[:, 2:4], ALU.max))
                    link(V.reciprocal(wv[:, 2:4], wv[:, 2:4]))
                    for r in range(2):
                        last = V.tensor_scalar(M["hs"][:, c, 2 * hp + r, :], P[:, 2 * hp + 1, r * VA:r * VA + DV], wv[:, 2 + r:3 + r], None, ALU.mult)
                    last.then_inc(E["st_new"], 1)
            dve.wait_ge(E["st_new"], 2 * TT)
            hs2 = view(R, KT * NCT + 4 * TOK + TOK + TT * 128, 16, DV)
            hsf = M["hs"].rearrange("p t h v -> p (t h) v")
            link(V.tensor_tensor(hs2, hsf, hsf, ALU.mult))
            link(V.tensor_reduce(SM[:, 160:176], hs2, AX, ALU.add))
            V.tensor_scalar(SM[:, 160:176], SM[:, 160:176], 1.0 / DV, EPS, ALU.mult, ALU.add).then_inc(E["hs_ms"], 1)
            dve.wait_ge(E["hs_rt"], 1)
            link(V.reciprocal(SM[:, 160:176], SM[:, 160:176]))
            dve.wait_ge(E["sog_scaled"], NT)
            for c in range(TT):
                for h in range(BH):
                    j = c * BH + h
                    last = V.scalar_tensor_tensor(out=M["hs"][:, c, h, :], in0=M["hs"][:, c, h, :], scalar=SM[:, 160 + j:161 + j], in1=sog[:, c, h * 128:(h + 1) * 128],
                                                  op0=ALU.mult, op1=ALU.mult)
            last.then_inc(E["outb"], 1)

            g8 = va[0:NS_, TT, 128:136]
            S8 = lambda a, b: SM[0:NS_, a:b]
            V.scalar_tensor_tensor(out=S8(68, 72), in0=g8[:, 4:8], scalar=-1.0, in1=g8[:, 4:8], op0=ALU.mult, op1=ALU.max).then_inc(E["sm_row"], 1)
            dve.wait_ge(E["sm_exp"], 1)
            dve.wait_ge(E["m0_in"], 16)
            link(V.scalar_tensor_tensor(out=S8(68, 72), in0=g8[:, 4:8], scalar=0.0, in1=S8(68, 72), op0=ALU.min, op1=ALU.subtract))
            link(V.tensor_tensor(S8(88, 92), S8(68, 72), S8(64, 68), ALU.add))
            link(V.tensor_tensor(S8(84, 88), S8(88, 92), g8[:, 0:4], ALU.max))
            V.tensor_tensor(S8(72, 76), g8[:, 0:4], S8(84, 88), ALU.subtract)
            V.tensor_tensor(S8(76, 80), S8(88, 92), S8(84, 88), ALU.subtract)
            V.tensor_scalar(S8(80, 84), S8(84, 88), -1.0, None, ALU.mult).then_inc(E["sm_row"], 1)
            dve.wait_ge(E["sm_exp"], 2)
            eye = ident[0:NS_, 0:NS_].unsqueeze(2).to_broadcast((NS_, NS_, BH))
            dve.wait_ge(E["outb_turned"], TT)
            for a in range(2):
                last = V.tensor_tensor(M["ew"][0:NS_, a, :].rearrange("p (b h) -> p b h", h=BH), S8(76 + 4 * a, 80 + 4 * a).unsqueeze(1).to_broadcast((NS_, NS_, BH)), eye, ALU.mult)
            last.then_inc(E["sm_w"], 1)
            dve.wait_ge(E["sm_k"], 1)
            dve.wait_ge(E["kt_outc"], 1)
            for h in range(BH):
                ins = V.tensor_scalar(M["sg"][0:NS_, 256 + h * 64:320 + h * 64], P[0:NS_, 0, h * 64:(h + 1) * 64], S8(72 + h, 73 + h), None, ALU.mult)
            link(ins)
            dve.wait_ge(E["sm_bc"], 1)
            link(V.tensor_copy(M["wk"].rearrange("p a j -> p (a j)"), P[:, 3, 0:64]))
            dve.wait_ge(E["c0_in"], 64)

            def add_out(g):
                t, hf, r = g // 2, g % 2, rows(g // 2)
                dve.wait_ge(E["wout"], g + 1)
                V.tensor_tensor(X[0:r, t, hf * 512:(hf + 1) * 512], X[0:r, t, hf * 512:(hf + 1) * 512], P[0:r, 4 + g % 4, :], ALU.add).then_inc(E["wout_added"], 1)

            for b in range(NS_ + 1):
                if b < NS_:
                    if b >= 2:
                        dve.wait_ge(E["sm_outer"], b - 1)
                    V.tensor_scalar(M["km"][0:NS_, b % 2, :], M["sg"][0:NS_, 256:512], ident[0:NS_, b:b + 1], None, ALU.mult).then_inc(E["sm_km"], 1)
                if b:
                    dve.wait_ge(E["sm_outer"], b)
                    for hp in range(2):
                        for r in range(2):
                            q, j = slice(r * 64, r * 64 + 64), (b - 1) * BH + 2 * hp + r
                            last = V.scalar_tensor_tensor(out=M["c0"][q, b - 1, hp, :], in0=M["c0"][q, b - 1, hp, :], scalar=M["wk"][q, 0, j:j + 1],
                                                          in1=P[q, 1 + (b - 1) % 2, hp * VA:(hp + 1) * VA], op0=ALU.mult, op1=ALU.add)
                    last.then_inc(E["sm_c1"], 1)
                if b % 2 and b < NS_:
                    add_out(b // 2)
            dve.wait_ge(E["sm_c1"], NS_)
            V.tensor_tensor(M["hst"][:, 0:16].rearrange("p (b h) -> p b h", h=2), M["c0"][:, :, :, DV], qc[:, 0:2, NP_:TOK].rearrange("p h b -> p b h"), ALU.mult).then_inc(E["sm_qn"], 1)
            add_out(4)
            dve.wait_ge(E["sm_h"], 1)
            par = lambda v, r: v.rearrange("p (j r) -> p r j", r=2)[:, r, :]
            for r in range(2):
                V.tensor_tensor(par(M["rc"], r), P[:, 1 + r, 64:80], par(M["wk"][:, 1, :], r), ALU.max)
                last = V.scalar_tensor_tensor(out=par(M["hst"], r), in0=P[:, 1 + r, 64:80], scalar=-1.0, in1=par(M["wk"][:, 1, :], r), op0=ALU.mult, op1=ALU.max)
            link(last)
            link(V.tensor_tensor(M["rc"], M["rc"], M["hst"], ALU.max))
            link(V.reciprocal(M["rc"], M["rc"]))
            for r in range(2):
                last = V.tensor_tensor(par(M["hst"], r), par(P[:, 1 + r, 0:32], r), par(M["rc"], r), ALU.mult)
            link(last)
            V.tensor_tensor(M["sq"], M["hst"], M["hst"], ALU.mult).then_inc(E["sm_sqr"], 1)
            add_out(5)
            dve.wait_ge(E["sm_ss"], 1)
            V.tensor_scalar(M["sq"], P[:, 3, 64:96], 1.0 / DV, EPS, ALU.mult, ALU.add).then_inc(E["sm_ms"], 1)
            add_out(6)
            dve.wait_ge(E["sm_ex2"], 1)
            link(V.reciprocal(M["sq"], M["sq"]))
            link(V.tensor_tensor(M["hst"], M["hst"], M["sq"], ALU.mult))
            V.tensor_tensor(M["mix"][:, 4:8, NP_:TOK], M["hst"].rearrange("p (b h) -> p h b", h=BH), P[:, 0, 256:288].rearrange("p (h b) -> p h b", h=BH), ALU.mult).then_inc(E["sm_done"], 1)
            for g in range(7, 2 * NT):
                add_out(g)
            return link.n

        CONV_AT = [11, 12, 13, 14]
        norm0 = Norm(0, A["norm_mix"][0], M["ht"], M["hn"], M["gain"], AR[:, 0:D], False, lambda e, t: e.wait_ge(x_in[t], 16))

        bf16 = mybir.dt.bfloat16
        Q = {}

        def carve_q(at, **parts):
            for n, dims in parts.items():
                Q[n] = view(AR, at, *dims)
                at += int(np.prod(dims))
            return at

        carve_q(0, ht=(KT, TOK), hn=(2, D), gain=(D,))
        carve_q(0, onehot=(NT * NE * CAP // 2,))
        endq = carve_q(0, xg=(3, D), yb=(3, D), hid=(3, FT * CAP), sg=(FT * CAP,), xt=(KT * CAP,))
        endq = max(endq, KT * TOK + 3 * D)
        endq = carve_q(endq, wr=(KT, 36), rb=(36,), lg=(NT, 36), key=(NT, NE), eq=(NT, NE), oh1=(NT, NE), oh2=(NT, NE), rank=(NT, NE),
                       val=(NT * NE * 4 // 2,), m5=(12, NT), base=(NE,), slots=(2, NE), slotw=(6,), cnt=(4,))
        assert endq <= 10240, endq
        ONEHOT = Q["onehot"].bitcast(bf16).rearrange("p (t e s) -> p t e s", t=NT, e=NE)
        VAL = Q["val"].bitcast(bf16).rearrange("p (t e c) -> p t e c", t=NT, e=NE)
        SLOTS = Q["slots"].bitcast(i32)
        SLOTW = Q["slotw"].bitcast(u32)
        CNT = Q["cnt"].bitcast(i32)

        def ring(u):
            at = u * EXP
            return (view(R, at, KT, FF), view(R, at + KT * FF, KT, FF), view(R, at + 2 * KT * FF, FT, D))

        GUESTS = {u: -(-(NE - u) // 3) for u in range(3)}
        MATS = ("gate", "up", "down")

        def load_weights(sp, layer, e, u, loaded, freed, which=(0, 1, 2)):
            for i in which:
                n, dst = MATS[i], ring(u)[i]
                freed(i)
                src = A[f"w_expert_{n}"][layer, e] if isinstance(e, int) else A[f"w_expert_{n}"][layer, bass.ds(e, 1)].squeeze(0)
                src = src.rearrange("(k p) d -> p k d", p=128) if n == "down" else src.rearrange("(p k) f -> p k f", k=KT)
                sp.dma_start(dst, src).then_inc(loaded[f"{n}{u}"], 16)

        def moe_norm(layer):
            nothing = lambda e, t: None
            return Norm(1 + 2 * layer, A["norm_ffn"][layer], Q["ht"], Q["hn"], Q["gain"], AR[:, 0:D], True, nothing)

        def load_router(sp, layer):
            moe_norm(layer).sp(sp)
            sp.dma_start(Q["wr"][:, :, 0:NG], A["w_router_group"][layer].rearrange("(k p) g -> p k g", p=128)).then_inc(router_in, 16)
            for g in range(NG):
                sp.dma_start(Q["wr"][:, :, NG + g * EG:NG + (g + 1) * EG], A["w_router_expert"][layer, g].rearrange("(k p) e -> p k e", p=128)).then_inc(router_in, 16)
            sp.dma_start(Q["rb"][:, 0:NG], A["b_router_group"][layer:layer + 1].to_broadcast((128, NG))).then_inc(router_in, 16)
            sp.dma_start(Q["rb"][:, NG:36], A["b_router_expert"][layer:layer + 1].rearrange("a g e -> a (g e)").to_broadcast((128, NE))).then_inc(router_in, 16)

        PREFETCHED = [3, 4]

        def meet(pool):
            pool.sem_inc(pool_steps, 1)

        class Pass:
            PER = dict(gate_done=NE, up_done=NE, y_done=NE, hid_made=NE, gs_made=NE, sig_made=NE, xt_act=NE, xt_dve=NE, x_turned=NE,
                       y_act=NE, y_dve=NE, pass_done=1, slots_made=1, onehot_made=NG, slots_done=1, row_copied=2 * NE, fallen=1, step=3)

            def __init__(self, tag, loaded=None, layers_before=0):
                self.PER = dict(self.PER)
                self.s, self.layers_before = dict(loaded or {}), layers_before
                for u in range(3):
                    for n in MATS + ("gathered", "scattered"):
                        self.PER[f"{n}{u}"] = 16 * GUESTS[u]
                for n in self.PER:
                    if n not in self.s and not (loaded and n in ("fallen", "step")):
                        self.s[n] = pool_sem() if n[:-1] in ("gathered", "scattered") else sem(f"{tag}_{n}")

            def at(self, name, count, before):
                loads = self.layers_before * self.PER[name] if name[:-1] in MATS else 0
                return before * self.PER[name] + count + loads

            def load(self, sp, layer, e, u, before, wait, which=(0, 1, 2)):
                def freed(i):
                    if wait:
                        done = ("gate_done", "up_done", "y_done")[i]
                        sp.wait_ge(self.s[done], self.at(done, e - 2, before))
                load_weights(sp, layer, e, u, self.s, freed, which)

            def sp_first(self, sp, layer, before):
                for u in range(3):
                    self.load(sp, layer, u, u, before, False)

            def sp_rest(self, sp, layer, before):
                def step(e, u):
                    self.load(sp, layer, e, u, before, True, (0, 1))
                    self.load(sp, layer, e - 1, (u + 2) % 3, before, True, (2,))

                self.load(sp, layer, 3, 0, before, True, (0, 1))
                with sp.Fori(0, (NE - 5) // 3) as i:
                    for c in range(3):
                        step(i * 3 + (4 + c), (1 + c) % 3)
                step(NE - 1, (NE - 1) % 3)
                self.load(sp, layer, NE - 1, (NE - 1) % 3, before, True, (2,))

            def turn_x(self, pe, e, u, n, before, first=False):
                pe.wait_ge(self.s[f"gathered{u}"], self.at(f"gathered{u}", n * 16 + 16, before))
                if not first:
                    pe.wait_ge(self.s["xt_act"], self.at("xt_act", e, before))
                    pe.wait_ge(self.s["xt_dve"], self.at("xt_dve", e, before))
                xk = Q["xg"][0:CAP, u, :].rearrange("s (p k) -> s k p", k=KT)
                for k in range(KT):
                    last = nc.tensor.transpose(P[:, k // 4, (k % 4) * CAP:(k % 4 + 1) * CAP], xk[:, k, :], ident[0:CAP, 0:CAP])
                last.then_inc(self.s["x_turned"], 1)

            def gate_up(self, pe, e, u, n, before, first=False):
                pe.wait_ge(self.s["xt_act"], self.at("xt_act", e + 1, before))
                pe.wait_ge(self.s["xt_dve"], self.at("xt_dve", e + 1, before))
                xt = Q["xt"].rearrange("p (k s) -> p k s", k=KT)
                for w, bank, name, done, freed in ((ring(u)[0], 2, f"gate{u}", "gate_done", "gs_made"), (ring(u)[1], 3, f"up{u}", "up_done", "hid_made")):
                    pe.wait_ge(self.s[name], self.at(name, n * 16 + 16, before))
                    if not first:
                        pe.wait_ge(self.s[freed], self.at(freed, e, before))
                    for m in range(FT):
                        for k in range(KT):
                            last = nc.tensor.matmul(P[:, bank, m * CAP:(m + 1) * CAP], w[:, k, m * 128:(m + 1) * 128], xt[:, k, :],
                                                    start=(k == 0), stop=(k == KT - 1))
                    last.then_inc(self.s[done], 1)

            def down(self, pe, e, u, n, before, first=False):
                pe.wait_ge(self.s["hid_made"], self.at("hid_made", e + 1, before))
                pe.wait_ge(self.s[f"down{u}"], self.at(f"down{u}", n * 16 + 16, before))
                if not first:
                    pe.wait_ge(self.s["y_act"], self.at("y_act", e, before))
                    pe.wait_ge(self.s["y_dve"], self.at("y_dve", e, before))
                for hf in range(2):
                    for k in range(FT):
                        last = nc.tensor.matmul(P[0:CAP, 4 + hf, :], Q["hid"][:, u, k * CAP:(k + 1) * CAP], ring(u)[2][:, k, hf * 512:(hf + 1) * 512],
                                                start=(k == 0), stop=(k == FT - 1))
                last.then_inc(self.s["y_done"], 1)

            def pe(self, pe, before):
                for e in range(NE):
                    if e % EG == 0:
                        pe.wait_ge(self.s["onehot_made"], self.at("onehot_made", e // EG + 1, before))
                    for t in range(NT):
                        last = nc.tensor.matmul(P[0:CAP, 6, e * 4:e * 4 + 4], ONEHOT[:, t, e, :], VAL[:, t, e, :], start=(t == 0), stop=(t == NT - 1))
                last.then_inc(self.s["slots_done"], 1)
                self.turn_x(pe, 0, 0, 0, before, True)
                self.gate_up(pe, 0, 0, 0, before, True)
                self.turn_x(pe, 1, 1, 0, before)

                def three(i):
                    for c in range(3):
                        e, u = i * 3 + (1 + c), (1 + c) % 3
                        nx = (2 + c) % 3
                        self.gate_up(pe, e, u, i + (1 + c) // 3, before)
                        self.turn_x(pe, e + 1, nx, i + (2 + c) // 3, before)
                        self.down(pe, e - 1, c % 3, i, before, isinstance(i, int) and e == 1)

                three(0)
                with pe.Fori(1, (NE - 2) // 3) as i:
                    three(i)
                e = NE - 1
                self.gate_up(pe, e, e % 3, e // 3, before)
                self.down(pe, e - 1, (e - 1) % 3, (e - 1) // 3, before)
                self.down(pe, e, e % 3, e // 3, before)

            def copy_x(self, eng, e, before):
                who, bank = ("xt_act", 1) if eng is nc.scalar else ("xt_dve", 0)
                eng.wait_ge(self.s["x_turned"], self.at("x_turned", e + 1, before))
                dst, src = Q["xt"][:, bank * 4 * CAP:(bank + 1) * 4 * CAP], P[:, bank, 0:4 * CAP]
                (nc.scalar.activation(dst, src, ACT.Copy) if bank else nc.vector.tensor_copy(dst, src)).then_inc(self.s[who], 1)

            def copy_y(self, eng, e, u, n, before):
                who, hf = ("y_act", 1) if eng is nc.scalar else ("y_dve", 0)
                eng.wait_ge(self.s["y_done"], self.at("y_done", e + 1, before))
                if not (isinstance(n, int) and n == 0):
                    eng.wait_ge(self.s[f"scattered{u}"], self.at(f"scattered{u}", n * 16, before))
                dst, src = Q["yb"][0:CAP, u, hf * 512:(hf + 1) * 512], P[0:CAP, 4 + hf, :]
                (nc.scalar.activation(dst, src, ACT.Copy) if hf else nc.vector.tensor_copy(dst, src)).then_inc(self.s[who], 1)

            def sigmoid(self, act, e, u, before, first=False):
                act.wait_ge(self.s["gate_done"], self.at("gate_done", e + 1, before))
                if not first:
                    act.wait_ge(self.s["gs_made"], self.at("gs_made", e, before))
                nc.scalar.activation(Q["sg"], P[:, 2, 0:FT * CAP], ACT.Sigmoid).then_inc(self.s["sig_made"], 1)

            def hidden(self, dve, e, u, before, first=False):
                dve.wait_ge(self.s["sig_made"], self.at("sig_made", e + 1, before))
                h = Q["hid"][:, u, :]
                nc.vector.tensor_tensor(h, P[:, 2, 0:FT * CAP], Q["sg"], ALU.mult).then_inc(self.s["gs_made"], 1)
                dve.wait_ge(self.s["gs_made"], self.at("gs_made", e + 1, before))
                dve.wait_ge(self.s["up_done"], self.at("up_done", e + 1, before))
                nc.vector.tensor_tensor(h, h, P[:, 3, 0:FT * CAP], ALU.mult).then_inc(self.s["hid_made"], 1)

            def middle(self, eng, before, product):
                self.copy_x(eng, 0, before)
                product(eng, 0, 0, before, True)
                self.copy_x(eng, 1, before)

                def three(i):
                    for c in range(3):
                        e = i * 3 + (1 + c)
                        product(eng, e, (1 + c) % 3, before)
                        self.copy_x(eng, e + 1, before)
                        self.copy_y(eng, e - 1, c % 3, i, before)

                three(0)
                with eng.Fori(1, (NE - 2) // 3) as i:
                    three(i)
                e = NE - 1
                product(eng, e, e % 3, before)
                for x in (e - 1, e):
                    self.copy_y(eng, x, x % 3, x // 3, before)

            def move(self, pool, e, u, n, before, out):
                w, k = SLOTW[0:CAP, 3 * out + u:3 * out + u + 1], 1 if out else 0
                if out:
                    pool.wait_ge(self.s["y_act"], self.at("y_act", e + 1, before))
                    pool.wait_ge(self.s["y_dve"], self.at("y_dve", e + 1, before))
                src = SLOTS[0:CAP, k, e:e + 1] if isinstance(e, int) else SLOTS[0:CAP, k, bass.ds(e, 1)]
                meet(pool)
                nc.gpsimd.tensor_copy(w.bitcast(i32), src).then_inc(self.s["row_copied"], 1)
                done = (e + e + 5 if out else e + e - 2) if n is not None else e + 1
                pool.wait_ge(self.s["row_copied"], self.at("row_copied", done, before))
                meet(pool)
                off = bass.IndirectOffsetOnAxis(ap=w, axis=0)
                if out:
                    pool.indirect_dma_start(out=y_dram, out_offset=off, in_=Q["yb"][0:CAP, u, :], in_offset=None,
                                            bounds_check=YROWS - 1, oob_is_err=False).then_inc(self.s[f"scattered{u}"], 16)
                else:
                    pool.indirect_dma_start(out=Q["xg"][0:CAP, u, :], out_offset=None, in_=h_dram, in_offset=off,
                                            bounds_check=TOK - 1, oob_is_err=False).then_inc(self.s[f"gathered{u}"], 16)

            def gather_next(self, pool, e, u, before):
                pool.wait_ge(self.s["x_turned"], self.at("x_turned", e - 2, before))
                self.move(pool, e, u, 0, before, 0)

            def pool(self, pool, before):
                pool.wait_ge(self.s["slots_made"], self.at("slots_made", 1, before))
                for e in range(3):
                    self.move(pool, e, e, None, before, 0)
                with pool.Fori(0, (NE - 5) // 3) as i:
                    for u in range(3):
                        self.gather_next(pool, i * 3 + (3 + u), u, before)
                        self.move(pool, i * 3 + u, u, 0, before, 1)
                for e in range(NE - 5, NE):
                    if e + 3 < NE:
                        self.gather_next(pool, e + 3, e % 3, before)
                        self.move(pool, e, e % 3, 0, before, 1)
                    else:
                        self.last_out(pool, e, before)
                for u in range(3):
                    pool.wait_ge(self.s[f"scattered{u}"], self.at(f"scattered{u}", 16 * GUESTS[u], before))
                meet(pool)
                pool.sem_inc(self.s["pass_done"], 1)

            def last_out(self, pool, e, before):
                u = e % 3
                w = SLOTW[0:CAP, 3 + u:4 + u]
                pool.wait_ge(self.s["y_act"], self.at("y_act", e + 1, before))
                pool.wait_ge(self.s["y_dve"], self.at("y_dve", e + 1, before))
                meet(pool)
                nc.gpsimd.tensor_copy(w.bitcast(i32), SLOTS[0:CAP, 1, e:e + 1]).then_inc(self.s["row_copied"], 1)
                pool.wait_ge(self.s["row_copied"], self.at("row_copied", NE + e + 1, before))
                meet(pool)
                pool.indirect_dma_start(out=y_dram, out_offset=bass.IndirectOffsetOnAxis(ap=w, axis=0), in_=Q["yb"][0:CAP, u, :], in_offset=None,
                                        bounds_check=YROWS - 1, oob_is_err=False).then_inc(self.s[f"scattered{u}"], 16)

            def slots(self, dve, link, before):
                V = nc.vector
                for g in range(NG):
                    es = slice(g * EG, (g + 1) * EG)
                    for t in range(NT):
                        last = V.tensor_tensor(ONEHOT[:, t, es], count_row[:, 0:CAP].unsqueeze(1).to_broadcast((128, EG, CAP)),
                                               Q["rank"][:, t, es].unsqueeze(2).to_broadcast((128, EG, CAP)), ALU.is_equal)
                    last.then_inc(self.s["onehot_made"], 1)
                dve.wait_ge(self.s["slots_done"], self.at("slots_done", 1, before))
                p6 = P[0:CAP, 6, 0:4 * NE].rearrange("p (e c) -> p e c", c=4)
                base = Q["base"][0:CAP, :]
                link(V.tensor_scalar(base, p6[:, :, 2], -SKIP, SKIP, ALU.mult, ALU.add))
                link(V.tensor_tensor(base, base, p6[:, :, 0], ALU.add))
                link(V.tensor_tensor(base, base, p6[:, :, 1], ALU.add))
                V.tensor_copy(SLOTS[0:CAP, 0, :], base)
                V.tensor_tensor(SLOTS[0:CAP, 1, :], base, p6[:, :, 3], ALU.add).then_inc(self.s["slots_made"], 1)

        def moe_part(layer, final=False):
            part_begins()
            main_pass = Pass("main", weight_in, layer)
            more_pass = Pass("more")
            RE = {n: sem(n) for n in "logits g_arg g_exp w_arg w_exp picks ranks passes_made all_passed combined".split()}
            y_in = [sem(f"y_in{j}") for j in range(6)]
            G_, JUNK = R[:, 0:D], R[:, D:2 * D]
            fss, fms, frt, frr = (SM[:, i:i + NT] for i in (0, 8, 24, 32))
            if final:
                N4 = {n: sem("final_" + n) for n in "gain_in squares mean root made".split()}

            def moe_sp(sp, layer):
                for t in (NT - 2, NT - 1):
                    sp.wait_ge(n_stored[t % 2], moe_norm(layer).at_store(t))
                for m in range(PREFETCHED[layer], 9):
                    load_weights(sp, layer, m // 3, m // 3, weight_in, lambda i: None, (m % 3,))
                main_pass.sp_rest(sp, layer, 0)

                def again(before):
                    sp.wait_ge(more_pass.s["slots_made"], more_pass.at("slots_made", 1, before))
                    more_pass.sp_first(sp, layer, before)
                    more_pass.sp_rest(sp, layer, before)
                more(sp, layer, again)
                sp.wait_ge(RE["all_passed"], 1)
                if final:
                    sp.dma_start(G_, A["norm_final"].rearrange("(a d) -> a d", a=1).to_broadcast((128, D))).then_inc(N4["gain_in"], 16)
                for t in range(NT):
                    if t >= 3:
                        sp.wait_ge(RE["combined"], t - 2)
                    for k in range(2):
                        at = k * TOK + t * 128
                        sp.dma_start((Q["yb"] if k else Q["xg"])[0:rows(t), t % 3, :], y_dram[at:at + rows(t), :]).then_inc(y_in[3 * k + t % 3], 16)
                if final:
                    for t in range(NT):
                        sp.wait_ge(N4["made"], t + 1)
                        dst = O["y_prompt"][0, t * 128:(t + 1) * 128, :] if t < TT else O["y_sample"][:, 0, :]
                        out_dma(sp, dst, X[0:rows(t), t, :])
                    sp.wait_ge(out_sp, stores["sp"])
                    sp.wait_ge(out_pool, stores["pool"])

            def more(eng, layer, body):
                eng.wait_ge(RE["passes_made"], 1)
                left = eng.value_load(CNT[0:1, 0:1], min_val=0, max_val=PASSES)
                with eng.Fori(0, PASSES - 1) as j:
                    with eng.If(left > j):
                        body(j)

            def moe_pool(pool, layer):
                moe_norm(layer).pool_store(pool)
                main_pass.pool(pool, 0)
                pool.sem_inc(more_pass.s["pass_done"], 1)
                more(pool, layer, lambda before: more_pass.pool(pool, before))
                pool.sem_inc(RE["all_passed"], 1)

            def moe_pe(pe, layer):
                moe_norm(layer).pe(pe)
                pe.wait_ge(n_copied, (2 + 2 * layer) * HALVES)
                pe.wait_ge(router_in, 16 * 7 * (layer + 1))
                for t in range(NT):
                    r = rows(t)
                    for k in range(KT):
                        last = nc.tensor.matmul(P[0:r, 4, t * 36:(t + 1) * 36], Q["ht"][:, k, t * 128:t * 128 + r], Q["wr"][:, k, :], start=(k == 0), stop=(k == KT - 1))
                last.then_inc(RE["logits"], 1)
                pe.wait_ge(RE["picks"], 1)
                for t in range(NT + 1):
                    for s_ in range(min(t, NT - 1) + 1):
                        stop = s_ == min(t, NT - 1)
                        last = nc.tensor.matmul(P[:, 5, t * NE:(t + 1) * NE], before if s_ == t else ones, Q["key"][:, s_, :], start=(s_ == 0), stop=stop)
                last.then_inc(RE["ranks"], 1)
                main_pass.pe(pe, 0)
                more(pe, layer, lambda b: more_pass.pe(pe, b))

            def moe_act(act, layer):
                link = Chain(act, act_seq)
                link.n = act_links[0]
                n = moe_norm(layer)
                n.act(act, link)
                n.act_copies(act)
                act.wait_ge(RE["g_arg"], 1)
                nc.scalar.activation(Q["m5"].rearrange("p a t -> p (a t)")[:, 0:4 * NT], Q["m5"].rearrange("p a t -> p (a t)")[:, 0:4 * NT], ACT.Exp).then_inc(RE["g_exp"], 1)
                act.wait_ge(RE["w_arg"], 1)
                nc.scalar.activation(Q["m5"][:, 7, :], Q["m5"][:, 7, :], ACT.Exp).then_inc(RE["w_exp"], 1)
                main_pass.middle(act, 0, main_pass.sigmoid)
                more(act, layer, lambda b: more_pass.middle(act, b, more_pass.sigmoid))
                if final:
                    act.wait_ge(RE["all_passed"], 1)
                    for t in range(NT):
                        act.wait_ge(RE["combined"], t + 1)
                        r = rows(t)
                        link(nc.scalar.activation(JUNK[0:r, :], X[0:r, t, :], ACT.Square, accum_out=fss[0:r, t:t + 1]))
                    nc.scalar.activation(SM[:, 16:17], part[:, 0:1], ACT.Square).then_inc(N4["squares"], 1)
                    act.wait_ge(N4["mean"], 1)
                    nc.scalar.activation(frt, fms, ACT.Sqrt).then_inc(N4["root"], 1)
                act_links[0] = link.n

            def moe_dve(dve, layer):
                V = nc.vector
                link = Chain(dve, dve_seq)
                link.n = dve_links[0]
                moe_norm(layer).dve(dve, link)
                lg, m5, key, eq, oh1, oh2, rank = (Q[x] for x in "lg m5 key eq oh1 oh2 rank".split())
                gl, el = lg[:, :, 0:NG], lg[:, :, NG:36]
                bc = lambda v, n: v.unsqueeze(2).to_broadcast((128, NT, n))
                ge = m5[:, 0:4, :].rearrange("p a t -> p (a t)").rearrange("p (t g) -> p t g", g=NG)
                dve.wait_ge(RE["logits"], 1)
                link(V.memset(lg, 0.0))
                p4 = P[:, 4, 0:NT * 36].rearrange("p (t c) -> p t c", t=NT)
                V.tensor_tensor(lg[:, 0:TT, :], p4[:, 0:TT, :], Q["rb"].unsqueeze(1).to_broadcast((128, TT, 36)), ALU.add)
                link(V.tensor_tensor(lg[0:NS_, TT, :], p4[0:NS_, TT, :], Q["rb"][0:NS_, :], ALU.add))
                first = Q["base"]
                V.tensor_scalar(first, count_row[:, 0:NE], -1.0, 64.0, ALU.mult, ALU.add)
                link(V.tensor_reduce(m5[:, 4, :], gl, AX, ALU.max))

                def pick(vals, top, n, out):
                    k, q = key[:, :, 0:n], eq[:, :, 0:n]
                    link(V.tensor_tensor(q, vals, bc(top, n), ALU.is_equal))
                    link(V.tensor_tensor(k, q, first[:, 0:n].unsqueeze(1).to_broadcast((128, NT, n)), ALU.mult))
                    link(V.tensor_reduce(m5[:, 9, :], k, AX, ALU.max))
                    link(V.tensor_tensor(out, k, bc(m5[:, 9, :], n), ALU.is_equal))

                V.tensor_tensor(ge, gl, bc(m5[:, 4, :], NG), ALU.subtract).then_inc(RE["g_arg"], 1)
                pick(gl, m5[:, 4, :], NG, rank[:, :, 0:NG])
                grp = rank[:, :, 0:NG]
                em = oh2
                split = lambda v: v.rearrange("p t (g e) -> p t g e", g=NG)
                for g in range(NG):
                    link(V.tensor_tensor(em[:, :, g * EG:(g + 1) * EG], el[:, :, g * EG:(g + 1) * EG], bc(rank[:, :, g], EG), ALU.mult))
                link(V.tensor_scalar(eq[:, :, 0:NG], grp, BIG, -BIG, ALU.mult, ALU.add))
                for g in range(NG):
                    link(V.tensor_tensor(em[:, :, g * EG:(g + 1) * EG], em[:, :, g * EG:(g + 1) * EG], bc(eq[:, :, g], EG), ALU.add))
                link(V.tensor_reduce(m5[:, 5, :], em, AX, ALU.max))
                pick(em, m5[:, 5, :], NE, oh1)
                link(V.scalar_tensor_tensor(out=em, in0=oh1, scalar=-BIG, in1=em, op0=ALU.mult, op1=ALU.add))
                link(V.tensor_reduce(m5[:, 6, :], em, AX, ALU.max))
                V.tensor_tensor(m5[:, 7, :], m5[:, 6, :], m5[:, 5, :], ALU.subtract).then_inc(RE["w_arg"], 1)
                pick(em, m5[:, 6, :], NE, oh2)
                link(V.tensor_scalar(oh1[:, TT, :], oh1[:, TT, :], samp, None, ALU.mult))
                link(V.tensor_scalar(oh2[:, TT, :], oh2[:, TT, :], samp, None, ALU.mult))
                V.tensor_tensor(key, oh1, oh2, ALU.add).then_inc(RE["picks"], 1)
                V.tensor_copy(VAL[:, :, :, 0], part.unsqueeze(2).to_broadcast((128, NT, NE)))
                for t in range(NT):
                    V.memset(VAL[:, t, :, 1], 128.0 * t)
                V.memset(VAL[:, :, :, 2], 1.0)
                V.tensor_scalar(VAL[:, :, :, 3], oh2, float(TOK), None, ALU.mult)
                dve.wait_ge(RE["ranks"], 1)
                dve.wait_ge(RE["picks"], 1)
                p5 = P[:, 5, 0:NT * NE].rearrange("p (t e) -> p t e", t=NT)
                link(V.scalar_tensor_tensor(out=rank, in0=p5, scalar=1.0, in1=key, op0=ALU.add, op1=ALU.mult))
                link(V.tensor_scalar(rank, rank, -1.0, None, ALU.add))
                link(V.tensor_reduce(m5[:, 10, 0:1], P[:, 5, NT * NE:(NT + 1) * NE], AX, ALU.max))
                link(V.tensor_scalar(key[:, 0, 0:PASSES - 1], count_row[:, 0:PASSES - 1], float(CAP), float(CAP), ALU.mult, ALU.add))
                link(V.tensor_scalar(key[:, 0, 0:PASSES - 1], key[:, 0, 0:PASSES - 1], m5[:, 10, 0:1], None, ALU.is_lt))
                link(V.tensor_reduce(m5[:, 10, 1:2], key[:, 0, 0:PASSES - 1], AX, ALU.add))
                V.tensor_copy(CNT[:, 0:1], m5[:, 10, 1:2]).then_inc(RE["passes_made"], 1)
                for t in (NT - 2, NT - 1):
                    dve.wait_ge(n_stored[t % 2], moe_norm(layer).at_store(t))
                main_pass.slots(dve, link, 0)
                dve.wait_ge(RE["g_exp"], 1)
                dve.wait_ge(RE["w_exp"], 1)
                link(V.tensor_reduce(m5[:, 8, :], ge, AX, ALU.add))
                link(V.reciprocal(m5[:, 8, :], m5[:, 8, :]))
                link(V.tensor_scalar(m5[:, 9, :], m5[:, 7, :], 1.0, None, ALU.add))
                link(V.reciprocal(m5[:, 9, :], m5[:, 9, :]))
                link(V.tensor_tensor(m5[:, 8, :], m5[:, 8, :], m5[:, 9, :], ALU.mult))
                link(V.tensor_tensor(m5[:, 9, :], m5[:, 8, :], m5[:, 7, :], ALU.mult))
                main_pass.middle(dve, 0, main_pass.hidden)

                def again(b):
                    dve.wait_ge(main_pass.s["pass_done"], 1)
                    dve.wait_ge(more_pass.s["pass_done"], b + 1)
                    V.tensor_scalar(rank, rank, -float(CAP), None, ALU.add).then_inc(more_pass.s["fallen"], 1)
                    dve.wait_ge(more_pass.s["fallen"], more_pass.at("fallen", 1, b))
                    more_pass.slots(dve, MoreLink(dve, b), b)
                    more_pass.middle(dve, b, more_pass.hidden)
                more(dve, layer, again)
                for t in range(NT):
                    r = rows(t)
                    for k in range(2):
                        n_on = t // 3 + 1
                        dve.wait_ge(y_in[3 * k + t % 3], 16 * n_on)
                        ins = V.scalar_tensor_tensor(out=X[0:r, t, :], in0=(Q["yb"] if k else Q["xg"])[0:r, t % 3, :], scalar=m5[0:r, 8 + k, t:t + 1], in1=X[0:r, t, :],
                                                     op0=ALU.mult, op1=ALU.add)
                        if k == 0:
                            link(ins)
                    ins.then_inc(RE["combined"], 1)
                if final:
                    dve.wait_ge(N4["squares"], 1)
                    V.tensor_scalar(fms, fss, 1.0 / D, EPS, ALU.mult, ALU.add).then_inc(N4["mean"], 1)
                    dve.wait_ge(N4["root"], 1)
                    link(V.reciprocal(frr, frt))
                    dve.wait_ge(N4["gain_in"], 16)
                    for t in range(NT):
                        r = rows(t)
                        V.scalar_tensor_tensor(out=X[0:r, t, :], in0=X[0:r, t, :], scalar=frr[0:r, t:t + 1], in1=G_[0:r, :], op0=ALU.mult, op1=ALU.mult).then_inc(N4["made"], 1)
                dve_links[0] = link.n

            class MoreLink:
                def __init__(self, eng, b):
                    self.eng, self.b, self.n = eng, b, 0

                def __call__(self, ins):
                    self.n += 1
                    ins.then_inc(more_pass.s["step"], 1)
                    self.eng.wait_ge(more_pass.s["step"], more_pass.at("step", self.n, self.b))

            with nc.Block() as block:
                @block.sync
                def _(sp):
                    moe_sp(sp, layer)

                @block.gpsimd
                def _(pool):
                    moe_pool(pool, layer)

                @block.scalar
                def _(act):
                    moe_act(act, layer)

                @block.tensor
                def _(pe):
                    moe_pe(pe, layer)

                @block.vector
                def _(dve):
                    moe_dve(dve, layer)
            part_ends()

        CT = D // 128
        TAPS_PE, TAPS_POOL = 4, 7
        TAPS_DVE = CK - TAPS_PE - TAPS_POOL
        ROW0 = CK - 1
        C = {}

        def carve_c(t, at, **parts):
            for n, dims in parts.items():
                C[n] = view(t, at, *dims)
                at += int(np.prod(dims))
            return at

        NV = CK + 5
        W1 = view(R, 0, KT, 2 * D)
        W2 = view(R, KT * 2 * D, KT, D)
        endc = carve_c(R, KT * 3 * D, y=(CT, TOK), diag=(CT, TAPS_PE, 128), strows=(2, D), prod=(NS_, CT, ROW0))
        assert endc <= 3 * EXP, (endc, 3 * EXP)
        C["vrows"] = C["y"].rearrange("p a b -> p (a b)")[:, 0:D]
        C["sig"] = C["strows"]
        C["term"] = C["prod"].rearrange("p a b c -> p (a b c)")[:, 0:3 * NP_].rearrange("p (a n) -> p a n", a=3)
        C["acc"] = C["strows"][:, :, NP_:2 * NP_]
        flat = C["diag"].rearrange("p a b c -> p (a b c)")
        C["sq"] = flat[:, 0:2 * D].rearrange("p (b k n) -> p b k n", b=2, k=CT)
        C["sw"] = flat[:, 2 * D:4 * D].rearrange("p (b k n) -> p b k n", b=2, k=CT)
        C["stat"] = C["prod"].rearrange("p a b c -> p (a b c)")[:, 0:4 * 128].rearrange("p (b a n) -> p b a n", b=2, a=2)
        endc = carve_c(AR, 0, ht=(KT, TOK), ext=(CT, ROW0 + NP_), gain=(D,), vec=(CT, NV), us=(CT, NS_), ys=(CT, NS_))
        assert endc <= 10240, endc
        C["hn"] = C["ext"].rearrange("p a b -> p (a b)")[:, 0:2 * D].rearrange("p (a d) -> p a d", a=2)
        C["b2"] = C["gain"]
        C["pout"] = C["ht"].rearrange("p a b -> p (a b)")[:, 0:D]
        C["sout"] = C["ht"].rearrange("p a b -> p (a b)")[:, D:2 * D]
        C["gs"] = C["sig"][:, 0, 0:CT * NS_].rearrange("p (c b) -> p c b", c=CT)

        def conv_part():
            part_begins()
            F = {n: sem("cv_" + n) for n in """vec_in st_in w1a_in w1b_in w2_in b2_in vec_turned vec_copied st_turned st_used pad_set
                 diag_made glu_done sig_made u_made us_arg us_sig us_made taps_done taps_used out_turned out_copied
                 mean_done centred squared var_done var_made rooted arg_made swish_sig z_made pw_done pw_added biased ys_made ys_summed term_made term_used acc_used""".split()}
            norm = Norm(2, A["norm_mix"][1], C["ht"], C["hn"], C["gain"], AR[:, 0:D], False, lambda e, t: None)
            w1 = A["w_pw1"][0].rearrange("(k p) n -> p k n", p=128)
            vec = C["vec"]
            tap = lambda c, j: vec[:, c, j:j + 1]
            bdw, lng, lnb, ba, bg = (vec[:, :, CK + i] for i in range(5))
            HALF = D // 2
            st_conv = A["state_conv"][0]

            def cols(t):
                return slice(t * 128, t * 128 + rows(t))

            with nc.Block() as block:
                @block.gpsimd
                def _(pool):
                    G = nc.gpsimd
                    out_dma(pool, O["s_conv"][0, :, 0:CK - 2, :], st_conv[:, 1:CK - 1, :])
                    pool.wait_ge(n_turned, 3 * HALVES)
                    G.memset(C["ext"][:, :, 0:ROW0], 0.0).then_inc(F["pad_set"], 1)
                    pool.wait_ge(F["vec_copied"], 1)
                    for c in range(CT):
                        G.tensor_tensor(C["diag"][:, c], ident.unsqueeze(1).to_broadcast((128, TAPS_PE, 128)),
                                        vec[:, c, CK - TAPS_PE:CK].unsqueeze(2).to_broadcast((128, TAPS_PE, 128)), ALU.mult).then_inc(F["diag_made"], 1)
                    pool.wait_ge(n_h_ready, 3 * NT)
                    pool.wait_ge(F["b2_in"], 16)
                    for t in range(NT):
                        r = rows(t)
                        G.tensor_tensor(X[0:r, t, :], X[0:r, t, :], C["b2"][0:r, :], ALU.add).then_inc(F["biased"], 1)
                    for c in range(CT):
                        if c >= 2:
                            pool.wait_ge(F["acc_used"], c - 1)
                        acc = C["acc"][:, c % 2, :]
                        for j in range(1, TAPS_POOL):
                            m = c * TAPS_POOL + j
                            pool.wait_ge(F["term_made"], m + 1)
                            if j > 1:
                                pool.wait_ge(F["term_used"], m)
                            old = C["term"][:, (m - 1) % 3, :] if j == 1 else acc
                            G.tensor_tensor(acc, old, C["term"][:, m % 3, :], ALU.add).then_inc(F["term_used"], 2 if j == 1 else 1)
                    pool.wait_ge(F["out_copied"], 1)
                    out_dma(pool, O["p_conv"][0, 0], C["pout"][0:ROW0, :])
                    out_dma(pool, O["s_conv"][0, :, CK - 2, :], C["sout"][0:NS_, :])
                    pool.wait_ge(out_pool, stores["pool"])

                @block.sync
                def _(sp):
                    norm.sp(sp)
                    V_ = C["vrows"]
                    sp.dma_start(V_[0:CK, :], A["w_dw"][0]).then_inc(F["vec_in"], 16)
                    for i, n in enumerate(("b_dw", "ln_conv_g", "ln_conv_b")):
                        sp.dma_start(V_[CK + i:CK + i + 1, :], A[n]).then_inc(F["vec_in"], 16)
                    sp.dma_start(V_[CK + 3:CK + 5, :], A["b_pw1"][0].rearrange("(a d) -> a d", a=2)).then_inc(F["vec_in"], 16)
                    for hf, n in enumerate(("w1a_in", "w1b_in")):
                        for g in range(2):
                            cs = slice(g * D + hf * HALF, g * D + (hf + 1) * HALF)
                            sp.dma_start(W1[:, :, cs], w1[:, :, cs]).then_inc(F[n], 16)
                        if hf == 0:
                            for j in range(2):
                                sp.dma_start(C["strows"][0:4 * ROW0, j, :], st_conv[4 * j:4 * j + 4].rearrange("b k c -> (b k) c")).then_inc(F["st_in"], 16)
                    sp.dma_start(W2, A["w_pw2"][0].rearrange("(k p) n -> p k n", p=128)).then_inc(F["w2_in"], 16)
                    sp.wait_ge(n_h_ready, 3 * NT)
                    sp.dma_start(C["b2"], A["b_pw2"].to_broadcast((128, D))).then_inc(F["b2_in"], 16)
                    sp.wait_ge(F["glu_done"], CT)
                    load_weights(sp, 1, 0, 0, weight_in, lambda i: None)
                    load_weights(sp, 1, 1, 1, weight_in, lambda i: None, (0,))
                    sp.wait_ge(F["biased"], NT)
                    sp.wait_ge(F["pw_done"], 2 * NT)
                    load_router(sp, 1)

                @block.tensor
                def _(pe):
                    norm.pe(pe)
                    pe.wait_ge(F["vec_in"], 16 * 5)
                    for c in range(CT):
                        last = nc.tensor.transpose(P[:, 4, c * NV:(c + 1) * NV], C["vrows"][0:NV, c * 128:(c + 1) * 128], ident[0:NV, 0:NV])
                    last.then_inc(F["vec_turned"], 1)
                    HT = C["ht"]
                    pe.wait_ge(n_copied, 3 * HALVES)
                    pe.wait_ge(F["vec_copied"], 1)

                    def glu(c):
                        if c % 4 == 0:
                            pe.wait_ge(F["w1b_in" if c else "w1a_in"], 32)
                        if c >= 2:
                            pe.wait_ge(F["u_made"], c - 1)
                        for g in range(2):
                            for k in range(KT):
                                w = W1[:, k, g * D + c * 128:g * D + (c + 1) * 128]
                                nc.tensor.matmul(P[:, 4, g * 64 + c * NS_:g * 64 + (c + 1) * NS_], w, HT[:, k, NP_:TOK], start=(k == 0), stop=(k == KT - 1))
                            for k in range(KT):
                                w = W1[:, k, g * D + c * 128:g * D + (c + 1) * 128]
                                last = nc.tensor.matmul(P[:, 2 * (c % 2) + g, :], w, HT[:, k, 0:NP_], start=(k == 0), stop=(k == KT - 1))
                        last.then_inc(F["glu_done"], 1)

                    def taps(c):
                        pe.wait_ge(F["u_made"], c + 1)
                        pe.wait_ge(F["diag_made"], c + 1)
                        if c == 0:
                            pe.wait_ge(F["st_used"], CT // 2)
                            pe.wait_ge(F["pad_set"], 1)
                        if c >= 2:
                            pe.wait_ge(F["taps_used"], c - 1)
                        for j in range(TAPS_PE):
                            at = CK - TAPS_PE + j
                            last = nc.tensor.matmul(P[:, 5 + c % 2, :], C["diag"][:, c, j, :], C["ext"][:, c, at:at + NP_], start=(j == 0), stop=(j == TAPS_PE - 1))
                        last.then_inc(F["taps_done"], 1)

                    glu(0)
                    pe.wait_ge(F["st_in"], 32)
                    for i in range(CT // 2):
                        if i == 3:
                            pe.wait_ge(F["st_used"], 1)
                        for c in (2 * i, 2 * i + 1):
                            for j in range(2):
                                last = nc.tensor.transpose(P[:, 5 + i % 3, (2 * (c % 2) + j) * 120:(2 * (c % 2) + j + 1) * 120],
                                                           C["strows"][0:120, j, c * 128:(c + 1) * 128], ident[0:120, 0:120])
                        last.then_inc(F["st_turned"], 1)
                    glu(1)
                    for p in range(1, CT // 2):
                        glu(2 * p)
                        glu(2 * p + 1)
                        taps(2 * p - 2)
                        taps(2 * p - 1)
                    taps(CT - 2)
                    taps(CT - 1)
                    pe.wait_ge(F["us_made"], 1)
                    pe.wait_ge(F["u_made"], CT)
                    for c in range(CT):
                        nc.tensor.transpose(P[0:ROW0, c // 4, (c % 4) * 128:(c % 4 + 1) * 128], C["ext"][:, c, NP_:NP_ + ROW0], ident)
                        last = nc.tensor.transpose(P[0:NS_, 2 + c // 4, (c % 4) * 128:(c % 4 + 1) * 128], C["us"][:, c, :], ident)
                    last.then_inc(F["out_turned"], 1)

                    def mean(t):
                        if t == 0:
                            pe.wait_ge(F["out_copied"], 1)
                            pe.wait_ge(F["acc_used"], CT)
                        if t == TT:
                            pe.wait_ge(F["ys_made"], 1)
                        if t >= 2:
                            pe.wait_ge(F["centred"], t - 1)
                        for k in range(CT):
                            last = nc.tensor.matmul(P[:, t % 2, 0:rows(t)], ones, C["y"][:, k, cols(t)], start=(k == 0), stop=(k == CT - 1))
                        last.then_inc(F["mean_done"], 1)

                    def variance(t):
                        pe.wait_ge(F["squared"], t + 1)
                        if t >= 2:
                            pe.wait_ge(F["var_made"], t - 1)
                        for k in range(CT):
                            last = nc.tensor.matmul(P[:, 2 + t % 2, 0:rows(t)], ones, C["sq"][:, t % 2, k, 0:rows(t)], start=(k == 0), stop=(k == CT - 1))
                        last.then_inc(F["var_done"], 1)

                    def project(t):
                        r = rows(t)
                        pe.wait_ge(F["z_made"], t + 1)
                        for hf in range(2):
                            g = 2 * t + hf
                            if g == 0:
                                pe.wait_ge(F["w2_in"], 16)
                                pe.wait_ge(F["taps_used"], CT)
                            if g >= 4:
                                pe.wait_ge(F["pw_added"], g - 3)
                            for k in range(CT):
                                last = nc.tensor.matmul(P[0:r, 4 + g % 4, :], C["y"][:, k, cols(t)], W2[:, k, hf * 512:(hf + 1) * 512], start=(k == 0), stop=(k == CT - 1))
                            last.then_inc(F["pw_done"], 1)

                    mean(0)
                    mean(1)
                    variance(0)
                    for t in range(NT):
                        if t + 2 < NT:
                            mean(t + 2)
                        if t + 1 < NT:
                            variance(t + 1)
                        project(t)

                @block.scalar
                def _(act):
                    link = Chain(act, act_seq)
                    link.n = act_links[0]
                    norm.act(act, link)
                    norm.act_copies(act)
                    act.wait_ge(F["vec_copied"], 1)
                    act.wait_ge(F["st_turned"], CT // 2)

                    def products(c):
                        for j in range(TAPS_POOL):
                            m = c * TAPS_POOL + j
                            if j == 0:
                                act.wait_ge(F["u_made"], c + 1)
                            if m >= 3:
                                act.wait_ge(F["term_used"], m - 2)
                            at = TAPS_DVE + j
                            nc.scalar.activation(C["term"][:, m % 3, :], C["ext"][:, c, at:at + NP_], ACT.Copy, scale=tap(c, at)).then_inc(F["term_made"], 1)

                    for c in range(CT):
                        act.wait_ge(F["glu_done"], c + 1)
                        if c >= 2:
                            act.wait_ge(F["u_made"], c - 1)
                        nc.scalar.activation(C["sig"][:, c % 2, 0:NP_], P[:, 2 * (c % 2) + 1, :], ACT.Sigmoid, bias=vec[:, c, CK + 4:CK + 5]).then_inc(F["sig_made"], 1)
                        if c == 1:
                            act.wait_ge(F["pad_set"], 1)
                            act.wait_ge(F["ys_summed"], 1)
                        if c == CT - 1:
                            act.wait_ge(F["us_arg"], 1)
                            nc.scalar.activation(C["gs"], C["gs"], ACT.Sigmoid).then_inc(F["us_sig"], 1)
                        if c:
                            products(c - 1)
                    products(CT - 1)
                    act.wait_ge(F["out_turned"], 1)
                    for j in range(2):
                        nc.scalar.activation(C["pout"][0:ROW0, j * 512:(j + 1) * 512], P[0:ROW0, j, :], ACT.Copy)
                        last = nc.scalar.activation(C["sout"][0:NS_, j * 512:(j + 1) * 512], P[0:NS_, 2 + j, :], ACT.Copy)
                    last.then_inc(F["out_copied"], 1)
                    for t in range(NT):
                        act.wait_ge(F["centred"], t + 1)
                        if t >= 2:
                            act.wait_ge(F["var_done"], t - 1)
                        nc.scalar.activation(C["sq"][:, t % 2, :, 0:rows(t)], C["y"][:, :, cols(t)], ACT.Square).then_inc(F["squared"], 1)
                        act.wait_ge(F["var_made"], t + 1)
                        st = C["stat"][:, t % 2, 1, 0:rows(t)]
                        nc.scalar.activation(st, st, ACT.Sqrt).then_inc(F["rooted"], 1)
                        act.wait_ge(F["arg_made"], t + 1)
                        if t >= 2:
                            act.wait_ge(F["z_made"], t - 1)
                        nc.scalar.activation(C["sw"][:, t % 2, :, 0:rows(t)], C["y"][:, :, cols(t)], ACT.Sigmoid).then_inc(F["swish_sig"], 1)
                    act_links[0] = link.n

                @block.vector
                def _(dve):
                    V = nc.vector
                    link = Chain(dve, dve_seq)
                    link.n = dve_links[0]
                    norm.dve(dve, link)
                    dve.wait_ge(F["vec_turned"], 1)
                    V.tensor_copy(vec, P[:, 4, 0:CT * NV].rearrange("p (c v) -> p c v", c=CT)).then_inc(F["vec_copied"], 1)
                    dve.wait_ge(F["vec_copied"], 1)
                    for i in range(CT // 2):
                        dve.wait_ge(F["st_turned"], i + 1)
                        for c in (2 * i, 2 * i + 1):
                            src = P[:, 5 + i % 3, (c % 2) * 240:(c % 2) * 240 + 240].rearrange("p (b k) -> p b k", b=NS_)
                            last = V.tensor_tensor(C["prod"][:, :, c, :], src, vec[:, c, 0:ROW0].unsqueeze(1).to_broadcast((128, NS_, ROW0)), ALU.mult)
                        last.then_inc(F["st_used"], 1)
                    dve.wait_ge(F["st_used"], CT // 2)
                    ys = C["ys"]
                    V.tensor_reduce(ys.rearrange("p c b -> p b c"), C["prod"], AX, ALU.add).then_inc(F["ys_summed"], 1)
                    dve.wait_ge(F["ys_summed"], 1)

                    def glu(c):
                        if c == 0:
                            dve.wait_ge(n_turned, 3 * HALVES)
                        dve.wait_ge(F["sig_made"], c + 1)
                        V.scalar_tensor_tensor(out=C["ext"][:, c, ROW0:ROW0 + NP_], in0=P[:, 2 * (c % 2), :], scalar=vec[:, c, CK + 3:CK + 4], in1=C["sig"][:, c % 2, 0:NP_],
                                               op0=ALU.add, op1=ALU.mult).then_inc(F["u_made"], 1)

                    def add_taps(c):
                        for x in (c, c + 1):
                            dve.wait_ge(F["taps_done"], x + 1)
                            y = C["y"][:, x, 0:NP_]
                            V.tensor_tensor(y, y, P[:, 5 + x % 2, :], ALU.add).then_inc(F["taps_used"], 1)
                        for x in (c, c + 1):
                            y = C["y"][:, x, 0:NP_]
                            dve.wait_ge(F["taps_used"], x + 1)
                            dve.wait_ge(F["term_used"], (x + 1) * TAPS_POOL)
                            V.tensor_tensor(y, y, C["acc"][:, x % 2, :], ALU.add).then_inc(F["acc_used"], 1)

                    def pair_taps(c):
                        dve.wait_ge(F["u_made"], c + 2)
                        for j in range(TAPS_DVE):
                            if c and j == 10:
                                dve.wait_ge(dve_seq, link.n)
                                add_taps(c - 2)
                            for x in (c, c + 1):
                                y, src = C["y"][:, x, 0:NP_], C["ext"][:, x, j:j + NP_]
                                if j == 0:
                                    ins = V.tensor_scalar(y, src, tap(x, 0), bdw[:, x:x + 1], ALU.mult, ALU.add)
                                else:
                                    ins = V.scalar_tensor_tensor(out=y, in0=src, scalar=tap(x, j), in1=y, op0=ALU.mult, op1=ALU.add)
                                link.n += 1
                                ins.then_inc(dve_seq, 1)
                                dve.wait_ge(dve_seq, link.n - 1)
                        dve.wait_ge(dve_seq, link.n)

                    glu(0)
                    glu(1)
                    dve.wait_ge(F["pad_set"], 1)
                    pair_taps(0)
                    for p in range(1, CT // 2):
                        glu(2 * p)
                        glu(2 * p + 1)
                        if p == CT // 2 - 1:
                            dve.wait_ge(F["glu_done"], CT)
                            us, gs = C["us"], C["gs"]
                            bc = lambda v: v.unsqueeze(2).to_broadcast((128, CT, NS_))
                            dve.wait_ge(F["u_made"], CT)
                            p4 = P[:, 4, 0:128].rearrange("p (g c b) -> p g c b", g=2, c=CT)
                            V.tensor_tensor(us, p4[:, 0], bc(ba), ALU.add)
                            V.tensor_tensor(gs, p4[:, 1], bc(bg), ALU.add).then_inc(F["us_arg"], 1)
                            dve.wait_ge(F["us_sig"], 1)
                            V.tensor_tensor(us, us, gs, ALU.mult).then_inc(F["us_made"], 1)
                            dve.wait_ge(F["us_made"], 1)
                            link(V.tensor_tensor(gs, us, bc(vec[:, :, CK - 1]), ALU.mult))
                            link(V.tensor_tensor(ys, ys, gs, ALU.add))
                            V.tensor_tensor(C["y"][:, :, NP_:TOK], ys, bc(bdw), ALU.add).then_inc(F["ys_made"], 1)
                        pair_taps(2 * p)
                    add_taps(CT - 2)
                    dve.wait_ge(F["acc_used"], CT)

                    def centre(t):
                        r, st = rows(t), C["stat"][:, t % 2]
                        y = C["y"][:, :, cols(t)]
                        dve.wait_ge(F["mean_done"], t + 1)
                        link(V.tensor_scalar(st[:, 0, 0:r], P[:, t % 2, 0:r], 1.0 / D, None, ALU.mult))
                        V.tensor_tensor(y, y, st[:, 0, 0:r].unsqueeze(1).to_broadcast((128, CT, r)), ALU.subtract).then_inc(F["centred"], 1)

                    def scale(t):
                        r, st = rows(t), C["stat"][:, t % 2]
                        y = C["y"][:, :, cols(t)]
                        dve.wait_ge(F["var_done"], t + 1)
                        V.tensor_scalar(st[:, 1, 0:r], P[:, 2 + t % 2, 0:r], 1.0 / D, EPS, ALU.mult, ALU.add).then_inc(F["var_made"], 1)
                        dve.wait_ge(F["rooted"], t + 1)
                        link(V.reciprocal(st[:, 1, 0:r], st[:, 1, 0:r]))
                        link(V.tensor_tensor(y, y, st[:, 1, 0:r].unsqueeze(1).to_broadcast((128, CT, r)), ALU.mult))
                        wide = lambda v: v.unsqueeze(2).to_broadcast((128, CT, r))
                        link(V.tensor_tensor(y, y, wide(lng), ALU.mult))
                        V.tensor_tensor(y, y, wide(lnb), ALU.add).then_inc(F["arg_made"], 1)

                    def swish(t):
                        y = C["y"][:, :, cols(t)]
                        dve.wait_ge(F["swish_sig"], t + 1)
                        V.tensor_tensor(y, y, C["sw"][:, t % 2, :, 0:rows(t)], ALU.mult).then_inc(F["z_made"], 1)

                    def residual(g):
                        t, hf, r = g // 2, g % 2, rows(g // 2)
                        if hf == 0:
                            dve.wait_ge(F["biased"], t + 1)
                        dve.wait_ge(F["pw_done"], g + 1)
                        x = X[0:r, t, hf * 512:(hf + 1) * 512]
                        V.tensor_tensor(x, x, P[0:r, 4 + g % 4, :], ALU.add).then_inc(F["pw_added"], 1)

                    centre(0)
                    for t in range(NT):
                        if t + 1 < NT:
                            centre(t + 1)
                        scale(t)
                        swish(t)
                        if t >= 1:
                            residual(2 * t - 2)
                            residual(2 * t - 1)
                    residual(2 * TT)
                    residual(2 * TT + 1)
                    dve_links[0] = link.n
            part_ends()

        with nc.Block() as block:
            @block.gpsimd
            def _(pool):
                mixer_pool(pool)

            @block.sync
            def _(sp):
                mixer_sp(sp)
                sp.wait_ge(E["wout"], 2 * NT)
                sp.wait_ge(E["sm_out"], 64)
                sp.wait_ge(out_pool, stores["pool"])
                load_router(sp, 0)
                load_weights(sp, 0, 0, 0, weight_in, lambda i: None)

            @block.scalar
            def _(act):
                act_links[0] = mixer_act(act)

            @block.tensor
            def _(pe):
                mixer_pe(pe)

            @block.vector
            def _(dve):
                dve_links[0] = mixer_dve(dve)
        part_ends()

        moe_part(0)
        conv_part()
        moe_part(1, final=True)


INS = ["x_prompt", "x_sample", "cache_win_k", "cache_win_v", "state_mlstm_c", "state_mlstm_n", "state_mlstm_m",
       "state_mlstm_conv", "state_conv", "norm_mix", "norm_ffn", "norm_final", "rel_bias_table", "w_in_mix",
       "b_mlstm_gates", "w_mlstm_qk_conv", "attn_sinks", "g_mlstm_norm", "w_out_mix", "w_pw1", "b_pw1", "w_dw", "b_dw",
       "ln_conv_g", "ln_conv_b", "w_pw2", "b_pw2", "w_router_group", "b_router_group", "w_router_expert",
       "b_router_expert", "w_expert_gate", "w_expert_up", "w_expert_down"]
OUTS = [("y_prompt", (1, NP_, D)), ("y_sample", (NS_, 1, D)),
        ("p_win_k", (1, 1, WIN, AKV, HD)), ("p_win_v", (1, 1, WIN, AKV, HD)), ("p_mlstm_c", (1, 1, BH, DK, DV)),
        ("p_mlstm_n", (1, 1, BH, DK)), ("p_mlstm_m", (1, 1, BH)), ("p_mlstm_conv", (1, 1, CONV - 1, 512)), ("p_conv", (1, 1, CK - 1, D)),
        ("s_win_k", (1, NS_, WIN, AKV, HD)), ("s_win_v", (1, NS_, WIN, AKV, HD)), ("s_mlstm_c", (1, NS_, BH, DK, DV)),
        ("s_mlstm_n", (1, NS_, BH, DK)), ("s_mlstm_m", (1, NS_, BH)), ("s_mlstm_conv", (1, NS_, CONV - 1, 512)),
        ("s_conv", (1, NS_, CK - 1, D))]


def kernel(**inputs):
    import concourse.bacc as bacc
    from concourse.bass_utils import run_bass_kernel_spmd
    nc = bacc.Bacc("TRN2", target_bir_lowering=False, num_devices=1)
    arrays, A, O = {}, {}, {}
    for name in INS:
        a = np.ascontiguousarray(inputs[name])
        arrays[f"in_{name}"] = a
        A[name] = nc.dram_tensor(f"in_{name}", a.shape, mybir.dt.from_np(a.dtype), kind="ExternalInput").ap()
    table = constants()
    for name, parts in (("keep", KEEP), ("mixc", MIXC)):
        a = np.ascontiguousarray(np.concatenate([table[n] for n in parts], axis=1).astype(np.float32))
        arrays[f"const_{name}"] = a
        A[name] = nc.dram_tensor(f"const_{name}", a.shape, mybir.dt.float32, kind="ExternalInput").ap()
    for name, shape in OUTS:
        O[name] = nc.dram_tensor(f"out_{name}", shape, mybir.dt.float32, kind="ExternalOutput").ap()
    build(nc, A, O)
    r = run_bass_kernel_spmd(nc, [arrays], core_ids=[0])
    return tuple(r.results[0][f"out_{name}"] for name, _ in OUTS)
```
